# Optimizing a Trainium2 kernel written in Bass

```python
import math
import jax, jax.numpy as jnp
from jax import lax
import numpy as np

D_MODEL = 1024
BATCH = 1
SEQ = 256
DEPTH = 2

N_MEM = 256
EPS = 1e-6
CONV_W = 512
CONV_K = 31
POOL_W = 512
POOL_GROUPS = 4
POOL_GW = POOL_W // POOL_GROUPS
POOL_WINDOWS = (2, 4, 8, 16)
MLSTM_W = 1024
MLSTM_HEADS = 4
MLSTM_DH = MLSTM_W // MLSTM_HEADS
MLSTM_CONV_K = 4
MLSTM_CHUNK = 64
N_BRANCH = 3
IN_COLS = 2 * CONV_W + POOL_W + 4 * MLSTM_W + 2 * MLSTM_HEADS + N_BRANCH * D_MODEL
XA_HEADS = 4
XA_DH = D_MODEL // XA_HEADS
D_FF = 2816
N_EXPERTS = 8
TOP_K = 2
D_FF_EXPERT = 3584
MOE_BLOCK = 128
N_DENSE = (DEPTH + 1) // 2
N_MOE = DEPTH // 2

kernel_name = "hybrid_conv_pool_mlstm_xattn_moe"

def rms_norm(x, g):
    x32 = x.astype(jnp.float32)
    y = x32 * lax.rsqrt(jnp.mean(x32 * x32, axis=-1, keepdims=True) + EPS)
    return (y * g.astype(jnp.float32)).astype(x.dtype)

def layer_norm(x, g, b):
    x32 = x.astype(jnp.float32)
    mu = jnp.mean(x32, axis=-1, keepdims=True)
    var = jnp.mean(jnp.square(x32 - mu), axis=-1, keepdims=True)
    y = (x32 - mu) * lax.rsqrt(var + EPS)
    return (y * g.astype(jnp.float32) + b.astype(jnp.float32)).astype(x.dtype)

def causal_depthwise_conv(u, w, b):
    K, C = w.shape
    y = lax.conv_general_dilated(
        u, w[:, None, :], window_strides=(1,), padding=[(K - 1, 0)],
        dimension_numbers=("NWC", "WIO", "NWC"), feature_group_count=C)
    return y + b

def causal_mean_minus_self(u, window):
    S = u.shape[1]
    cs = jnp.cumsum(u, axis=1)
    prev = jnp.pad(cs, ((0, 0), (window, 0), (0, 0)))[:, :S]
    cnt = jnp.minimum(jnp.arange(1, S + 1), window).astype(jnp.float32)
    return (cs - prev) / cnt[None, :, None] - u

def pool_mixer(u, pool_w, pool_scale):
    Bsz, S, _ = u.shape
    u32 = u.astype(jnp.float32).reshape(Bsz, S, POOL_GROUPS, POOL_GW)
    pooled = jnp.stack([causal_mean_minus_self(u32[:, :, g], POOL_WINDOWS[g])
                        for g in range(POOL_GROUPS)], axis=2)
    y = jnp.einsum("bsgc,gcd->bsgd", pooled, pool_w.astype(jnp.float32))
    y = y.reshape(Bsz, S, POOL_W) * pool_scale.astype(jnp.float32)
    return y.astype(u.dtype)

def mlstm_chunkwise(q, k, v, ig, lf):
    Bsz, H, S, dh = q.shape
    L = MLSTM_CHUNK
    nc = S // L

    def chunks(a):
        return jnp.moveaxis(a.reshape(Bsz, H, nc, L, *a.shape[3:]), 2, 0)

    causal = jnp.tril(jnp.ones((L, L), dtype=bool))

    def step(carry, xs):
        C, n, m = carry
        q_, k_, v_, i_, f_ = xs
        b = jnp.cumsum(f_, axis=-1)
        logD = b[..., :, None] - b[..., None, :] + i_[..., None, :]
        logD = jnp.where(causal, logD, -jnp.inf)
        inter = b + m[..., None]
        mt = jnp.maximum(inter, jnp.max(logD, axis=-1))
        Dm = jnp.exp(logD - mt[..., None])
        a_inter = jnp.exp(inter - mt)
        s = jnp.einsum("bhtd,bhsd->bhts", q_, k_) * Dm
        num = (jnp.einsum("bhts,bhse->bhte", s, v_)
               + a_inter[..., None] * jnp.einsum("bhed,bhtd->bhte", C, q_))
        den = jnp.sum(s, axis=-1) + a_inter * jnp.einsum("bhd,bhtd->bht", n, q_)
        h = num / jnp.maximum(jnp.abs(den), jnp.exp(-mt))[..., None]
        bL = b[..., -1]
        w_log = bL[..., None] - b + i_
        m_new = jnp.maximum(bL + m, jnp.max(w_log, axis=-1))
        a_c = jnp.exp(bL + m - m_new)
        w = jnp.exp(w_log - m_new[..., None])
        C_new = a_c[..., None, None] * C + jnp.einsum("bhs,bhse,bhsd->bhed", w, v_, k_)
        n_new = a_c[..., None] * n + jnp.einsum("bhs,bhsd->bhd", w, k_)
        return (C_new, n_new, m_new), h

    init = (jnp.zeros((Bsz, H, dh, dh), jnp.float32),
            jnp.zeros((Bsz, H, dh), jnp.float32),
            jnp.zeros((Bsz, H), jnp.float32))
    _, hs = lax.scan(step, init, (chunks(q), chunks(k), chunks(v), chunks(ig), chunks(lf)))
    return jnp.moveaxis(hs, 0, 2).reshape(Bsz, H, S, dh)

def hybrid_mixer(xn, w_in, b_in, conv_dw_w, conv_dw_b, conv_ln_g, conv_ln_b, w_conv_out,
                 pool_w, pool_scale, w_pool_out, mlstm_conv_w, mlstm_conv_b,
                 mlstm_norm_g, w_mlstm_out, w_out):
    Bsz, S, D = xn.shape
    dt = xn.dtype
    proj = xn @ w_in + b_in
    sizes = [CONV_W, CONV_W, POOL_W, MLSTM_W, MLSTM_W, MLSTM_W, MLSTM_W,
             MLSTM_HEADS, MLSTM_HEADS, N_BRANCH * D_MODEL]
    offs, acc = [], 0
    for sz in sizes[:-1]:
        acc += sz
        offs.append(acc)
    c_a, c_b, p_u, m_q, m_k, m_v, m_z, m_i, m_f, g_pre = jnp.split(proj, offs, axis=-1)

    u = c_a * jax.nn.sigmoid(c_b)
    u = causal_depthwise_conv(u, conv_dw_w, conv_dw_b)
    u = jax.nn.silu(layer_norm(u, conv_ln_g, conv_ln_b))
    y_a = u @ w_conv_out

    y_b = pool_mixer(p_u, pool_w, pool_scale) @ w_pool_out

    qk = jax.nn.silu(causal_depthwise_conv(jnp.concatenate([m_q, m_k], axis=-1),
                                           mlstm_conv_w, mlstm_conv_b))
    q, k = jnp.split(qk, 2, axis=-1)

    def heads(t):
        return t.reshape(Bsz, S, MLSTM_HEADS, MLSTM_DH).transpose(0, 2, 1, 3).astype(jnp.float32)

    ig = m_i.astype(jnp.float32).transpose(0, 2, 1)
    lf = jax.nn.log_sigmoid(m_f.astype(jnp.float32)).transpose(0, 2, 1)
    h = mlstm_chunkwise(heads(q), heads(k) * (MLSTM_DH ** -0.5), heads(v=m_v) if False else heads(m_v), ig, lf)
    h = h.transpose(0, 2, 1, 3)
    h = h * lax.rsqrt(jnp.mean(h * h, axis=-1, keepdims=True) + EPS)
    h = h * mlstm_norm_g.astype(jnp.float32).reshape(MLSTM_HEADS, MLSTM_DH)
    h = h.reshape(Bsz, S, MLSTM_W) * jax.nn.sigmoid(m_z.astype(jnp.float32))
    y_c = h.astype(dt) @ w_mlstm_out

    g = jax.nn.sigmoid(g_pre.astype(jnp.float32)).astype(dt).reshape(Bsz, S, N_BRANCH, D_MODEL)
    y = g[:, :, 0] * y_a + g[:, :, 1] * y_b + g[:, :, 2] * y_c
    return y @ w_out

def memory_cross_attention(hn, mem_n, wq, wk, wv, wo):
    Bsz, S, _ = hn.shape
    M = mem_n.shape[1]
    q = (hn @ wq).reshape(Bsz, S, XA_HEADS, XA_DH)
    k = (mem_n @ wk).reshape(Bsz, M, XA_HEADS, XA_DH)
    v = (mem_n @ wv).reshape(Bsz, M, XA_HEADS, XA_DH)
    s = jnp.einsum("bshd,bmhd->bhsm", q, k).astype(jnp.float32) * (XA_DH ** -0.5)
    p = jax.nn.softmax(s, axis=-1).astype(v.dtype)
    o = jnp.einsum("bhsm,bmhd->bshd", p, v).reshape(Bsz, S, XA_HEADS * XA_DH)
    return o @ wo

def swiglu(xn, w1, w3, w2):
    return (jax.nn.silu(xn @ w1) * (xn @ w3)) @ w2

def moe_swiglu(xn, router_w, w1, w3, w2):
    Bsz, S, D = xn.shape
    N = Bsz * S
    xt = xn.reshape(N, D)
    logits = (xt @ router_w).astype(jnp.float32)
    top_v, top_e = lax.top_k(logits, TOP_K)
    gate = jax.nn.softmax(top_v, axis=-1)
    A = N * TOP_K
    e_flat = top_e.reshape(A)
    tok_flat = jnp.repeat(jnp.arange(N, dtype=jnp.int32), TOP_K)
    w_flat = gate.reshape(A)
    order = jnp.argsort(e_flat)
    e_s, tok_s, w_s = e_flat[order], tok_flat[order], w_flat[order]
    counts = jnp.bincount(e_flat, length=N_EXPERTS)
    padded = (counts + MOE_BLOCK - 1) // MOE_BLOCK * MOE_BLOCK
    off = jnp.cumsum(counts) - counts
    ends = jnp.cumsum(padded)
    poff = ends - padded
    dest = poff[e_s] + (jnp.arange(A, dtype=jnp.int32) - off[e_s])
    n_blocks = -(-A // MOE_BLOCK) + N_EXPERTS
    P = n_blocks * MOE_BLOCK
    slot_tok = jnp.zeros((P,), jnp.int32).at[dest].set(tok_s)
    slot_w = jnp.zeros((P,), jnp.float32).at[dest].set(w_s)
    block_e = jnp.minimum(
        jnp.searchsorted(ends, jnp.arange(n_blocks) * MOE_BLOCK, side="right"), N_EXPERTS - 1)
    xb = xt[slot_tok].reshape(n_blocks, MOE_BLOCK, D)

    def expert_block(args):
        xblk, e = args
        return (jax.nn.silu(xblk @ w1[e]) * (xblk @ w3[e])) @ w2[e]

    yb = lax.map(expert_block, (xb, block_e)).reshape(P, D)
    y = jax.ops.segment_sum(yb * slot_w[:, None], slot_tok, num_segments=N)
    return y.reshape(Bsz, S, D).astype(xn.dtype)

def setup_inputs(seed: int = 0) -> dict:
    key = jax.random.key(seed)
    ks = iter(jax.random.split(key, 48))
    f32 = jnp.float32

    def nrm(shape, scale):
        return jax.random.normal(next(ks), shape, f32) * scale

    def gain(shape):
        return 1.0 + 0.05 * jax.random.normal(next(ks), shape, f32)

    D = D_MODEL
    f_off = 2 * CONV_W + POOL_W + 4 * MLSTM_W + MLSTM_HEADS
    b_in = nrm((DEPTH, IN_COLS), 0.02)
    b_in = b_in.at[:, f_off:f_off + MLSTM_HEADS].add(jnp.linspace(3.0, 6.0, MLSTM_HEADS))
    return {
        "x": nrm((BATCH, SEQ, D), 1.0),
        "mem": nrm((BATCH, N_MEM, D), 1.0),
        "mem_norm_g": gain((D,)),
        "norm_mix_g": gain((DEPTH, D)),
        "w_in": nrm((DEPTH, D, IN_COLS), D ** -0.5),
        "b_in": b_in,
        "conv_dw_w": nrm((DEPTH, CONV_K, CONV_W), CONV_K ** -0.5),
        "conv_dw_b": nrm((DEPTH, CONV_W), 0.02),
        "conv_ln_g": gain((DEPTH, CONV_W)),
        "conv_ln_b": nrm((DEPTH, CONV_W), 0.02),
        "w_conv_out": nrm((DEPTH, CONV_W, D), CONV_W ** -0.5),
        "pool_w": nrm((DEPTH, POOL_GROUPS, POOL_GW, POOL_GW), POOL_GW ** -0.5),
        "pool_scale": 1.0 + 0.1 * nrm((DEPTH, POOL_W), 1.0),
        "w_pool_out": nrm((DEPTH, POOL_W, D), POOL_W ** -0.5),
        "mlstm_conv_w": nrm((DEPTH, MLSTM_CONV_K, 2 * MLSTM_W), MLSTM_CONV_K ** -0.5),
        "mlstm_conv_b": nrm((DEPTH, 2 * MLSTM_W), 0.02),
        "mlstm_norm_g": gain((DEPTH, MLSTM_W)),
        "w_mlstm_out": nrm((DEPTH, MLSTM_W, D), MLSTM_W ** -0.5),
        "w_out": nrm((DEPTH, D, D), D ** -0.5),
        "norm_xattn_g": gain((DEPTH, D)),
        "xa_wq": nrm((DEPTH, D, XA_HEADS * XA_DH), D ** -0.5),
        "xa_wk": nrm((DEPTH, D, XA_HEADS * XA_DH), D ** -0.5),
        "xa_wv": nrm((DEPTH, D, XA_HEADS * XA_DH), D ** -0.5),
        "xa_wo": nrm((DEPTH, XA_HEADS * XA_DH, D), (XA_HEADS * XA_DH) ** -0.5),
        "norm_ffn_g": gain((DEPTH, D)),
        "ffn_w1": nrm((N_DENSE, D, D_FF), D ** -0.5),
        "ffn_w3": nrm((N_DENSE, D, D_FF), D ** -0.5),
        "ffn_w2": nrm((N_DENSE, D_FF, D), D_FF ** -0.5),
        "router_w": nrm((N_MOE, D, N_EXPERTS), D ** -0.5),
        "moe_w1": nrm((N_MOE, N_EXPERTS, D, D_FF_EXPERT), D ** -0.5),
        "moe_w3": nrm((N_MOE, N_EXPERTS, D, D_FF_EXPERT), D ** -0.5),
        "moe_w2": nrm((N_MOE, N_EXPERTS, D_FF_EXPERT, D), D_FF_EXPERT ** -0.5),
        "final_norm_g": gain((D,)),
    }

def reference(x, mem, mem_norm_g, norm_mix_g, w_in, b_in, conv_dw_w, conv_dw_b,
              conv_ln_g, conv_ln_b, w_conv_out, pool_w, pool_scale, w_pool_out,
              mlstm_conv_w, mlstm_conv_b, mlstm_norm_g, w_mlstm_out, w_out,
              norm_xattn_g, xa_wq, xa_wk, xa_wv, xa_wo, norm_ffn_g,
              ffn_w1, ffn_w3, ffn_w2, router_w, moe_w1, moe_w3, moe_w2, final_norm_g):
    mem_n = rms_norm(mem, mem_norm_g)
    h = x
    for l in range(DEPTH):
        h = h + hybrid_mixer(rms_norm(h, norm_mix_g[l]), w_in[l], b_in[l],
                             conv_dw_w[l], conv_dw_b[l], conv_ln_g[l], conv_ln_b[l],
                             w_conv_out[l], pool_w[l], pool_scale[l], w_pool_out[l],
                             mlstm_conv_w[l], mlstm_conv_b[l], mlstm_norm_g[l],
                             w_mlstm_out[l], w_out[l])
        h = h + memory_cross_attention(rms_norm(h, norm_xattn_g[l]), mem_n,
                                       xa_wq[l], xa_wk[l], xa_wv[l], xa_wo[l])
        hn = rms_norm(h, norm_ffn_g[l])
        j = l // 2
        if l % 2 == 0:
            h = h + swiglu(hn, ffn_w1[j], ffn_w3[j], ffn_w2[j])
        else:
            h = h + moe_swiglu(hn, router_w[j], moe_w1[j], moe_w3[j], moe_w2[j])
    return rms_norm(h, final_norm_g)


_drawn_inputs = setup_inputs


def setup_inputs(seed=0):
    import zlib

    import numpy as np

    out = dict(_drawn_inputs(seed))
    spreads = {}
    factors = {'conv_ln_b': 3.07, 'mlstm_conv_b': 3.34, 'norm_xattn_g': 3.297}
    for name, (base, spread) in spreads.items():
        noise = np.random.default_rng([zlib.crc32(name.encode()), seed]).standard_normal(out[name].shape)
        drawn = base * np.exp(spread * noise) if base else spread * noise
        out[name] = __import__('jax').numpy.asarray(drawn.astype(out[name].dtype))
    for name, factor in factors.items():
        out[name] = (out[name] * factor).astype(out[name].dtype)
    return out
```

```python
from contextlib import ExitStack

import concourse.bass as bass
from concourse import mybir

F32 = mybir.dt.float32
F32R = mybir.dt.float32r
I32 = mybir.dt.int32
ALU = mybir.AluOpType
ACT = mybir.ActivationFunctionType
AX = mybir.AxisListType.X

P = 128
T = 256
TT = T // P
D = 1024
KB = D // P
DEPTH = 2
EPS = 1e-6
CONV_W, CONV_K = 512, 31
CB = CONV_W // P
POOL_WINDOWS = (2, 4, 8, 16)
NG = len(POOL_WINDOWS)
MCONV_K = 4
HEADS = 4
DH = D // HEADS
D_FF = 2816
NE = 8
D_FFE = 3584
C_A, C_B, C_POOL, C_Q, C_K, C_V, C_Z, C_I, C_F, C_G = 0, 512, 1024, 1536, 2560, 3584, 4608, 5632, 5636, 5640

CH = 2048
RAW = 3
SPL = 3

AB0, QK0, V0, PU0, Z0, PW, GB0, WP0, GA0, WC0, GC0 = 0, 4, 12, 16, 18, 22, 23, 27, 29, 33, 35
WO0, XK0, XV0, XQ0, XV1, XO0, N_MIX = 43, 47, 51, 52, 56, 59, 63
N_FFG = D_FF // T
N_FF = 3 * N_FFG
FF_SEQ = [("up", g, i) for g in range(1) for i in range(2)]
for _g in range(1, N_FFG):
    FF_SEQ += [("up", _g, 0), ("up", _g, 1), ("down", _g - 1, 0)]
FF_SEQ.append(("down", N_FFG - 1, 0))
N_LAYER = N_MIX + N_FF
assert N_LAYER % RAW == 0 and N_LAYER % SPL == 0 and N_MIX % RAW == 0 and N_MIX % SPL == 0

FG = 512
NGE = D_FFE // FG
N_EXP = 6 * NGE
ERAW = 6
SLOTS = 128
N_OVER = (2 * T - 1) // (SLOTS + 1)
NBLK = NE + N_OVER
XW = NBLK + 1


def expert_chunks():
    seq = []
    for g in range(NGE):
        seq += [("w1", g, 0), ("w1", g, 1), ("w3", g, 0), ("w3", g, 1)]
        if g:
            seq += [("w2", g - 1, 0), ("w2", g - 1, 1)]
    return seq + [("w2", NGE - 1, 0), ("w2", NGE - 1, 1)]


ESEQ = expert_chunks()
assert len(ESEQ) == N_EXP and N_EXP % ERAW == 0 and N_EXP % SPL == 0
E_AT = {key: m for m, key in enumerate(ESEQ)}


def bank_plan():
    steps = [(("chunk", c), 1) for c in range(PW)] + [(("chunk", PW), 2)]
    steps += [(("chunk", c), 1) for c in range(GB0, WP0)] + [(("chunk", WP0), 2), (("chunk", WP0 + 1), 2)]
    steps += [(("chunk", GA0), 1), ("hidden_t", 4)]
    steps += [(("chunk", c), 1) for c in range(GA0 + 1, WC0)] + [(("chunk", WC0), 2), (("chunk", WC0 + 1), 2)]
    steps += [(("chunk", c), 1) for c in range(GC0, N_MIX)]
    plan, last, n = {}, [None] * 4, 0
    for key, count in steps:
        plan[key] = []
        for part in range(count):
            plan[key].append((n % 4, last[n % 4]))
            last[n % 4] = (key, part)
            n += 1
    return plan


PLAN = bank_plan()
CONSTS = 9
SCORES = (PW - 3, PW - 1, PW, PW + 1)
GATE_ROWS = QK0
LN_MEAN, LN_VAR, HIDDEN_T = WP0 + 1, GA0 + 1, GA0
X_OUT_AFTER = {XQ0 + 3: (0,), XV1 + 1: (1,), XO0 - 1: (2, 3)}
DVE_TAPS = {j: range(3 * (j - V0), min(3 * (j - V0) + 3, CONV_K)) for j in range(V0, V0 + (CONV_K + 2) // 3)}
HALF = T


class Signal:

    def __init__(self, ctx, nc, name, mixer, ffn=0, before=0):
        self.sem = ctx.enter_context(nc.semaphore(name))
        self.before, self.mixer, self.layer = before, mixer, mixer + ffn

    def at(self, layer, n):
        return layer * self.layer + (self.before + n)

    @property
    def moe(self):
        return self.before + self.layer + self.mixer


class Chain:

    def __init__(self, eng, sem, per_layer):
        self.eng, self.sem, self.per_layer, self.base, self.n = eng, sem, per_layer, 0, 0

    def did(self, ins):
        ins.then_inc(self.sem, 1)
        self.n += 1
        return self.n

    def need(self, n):
        self.eng.wait_ge(self.sem, self.base + n)

    def link(self, ins):
        self.need(self.did(ins))


def trunk(nc, w, out):
    ctx = ExitStack()
    with ctx:
        def sb(name, shape, dt=F32):
            return ctx.enter_context(nc.sbuf_tensor(name, shape, dt))

        def sem(name):
            return ctx.enter_context(nc.semaphore(name))

        def sig(name, mixer, ffn=0, before=0):
            return Signal(ctx, nc, name, mixer, ffn, before)

        raw = [sb(f"raw{i}", [P, CH]) for i in range(RAW)]
        w_hi = [sb(f"w_hi{i}", [P, CH], F32R) for i in range(SPL)]
        w_lo = [sb(f"w_lo{i}", [P, CH], F32R) for i in range(SPL)]
        a_hi, a_lo = sb("a_hi", [P, KB, T], F32R), sb("a_lo", [P, KB, T], F32R)
        b_hi, b_lo = sb("b_hi", [P, KB, T], F32R), sb("b_lo", [P, KB, T], F32R)
        h = sb("h", [P, KB, T])
        mem_t = sb("mem_t", [P, KB, T])
        xf = sb("xf", [P, KB, T])
        q_t, k_t = sb("q_t", [P, KB, T]), sb("k_t", [P, KB, T])
        vx = sb("vx", [P, TT, HEADS, DH + 1])
        z_sig = sb("z_sig", [P, KB, T])
        u_pad = sb("u_pad", [P, CB, CONV_K - 1 + T])
        c31 = sb("c31", [P, CB, T])
        area = sb("area", [P, 2120])
        cacc = sb("cacc", [P, 4, T])
        vb_pool = sb("vb_pool", [P, D])
        sgb = sb("sgb", [P, 2, T])
        rstd = sb("rstd", [P, 2, T])
        dec = sb("dec", [P, 2, 3 * P])
        wdk = sb("wdk", [P, 2, 3 * P])
        wif = sb("wif", [P, KB, 36])
        wif_hi, wif_lo = sb("wif_hi", [P, KB, 36], F32R), sb("wif_lo", [P, KB, 36], F32R)
        ident, ones = sb("ident", [P, P]), sb("ones", [P, P])
        selh = sb("selh", [HEADS, HEADS, P])
        rcnt = sb("rcnt", [P, NG, 16])
        prow = sb("prow", [P, 3, P])
        par = sb("par", [P, 3, P])
        if_bias = sb("if_bias", [36, 1])
        rows = z_sig[0:HEADS, 0:4, :]
        taps = xf[:, 0:4, :].rearrange("p (s c) t -> p s c t", s=2)
        m_row = sb("m_row", [HEADS, T])
        zrow = sb("zrow", [HEADS, T])
        gcols = sb("gcols", [P, 16])
        small = sb("small", [P, 64])
        xcols = sb("xcols", [P, 4, HEADS, TT])
        eps = sb("eps", [P, 1])

        pre = area[:, 0:4 * 259].rearrange("p (c t) -> p c t", c=4)
        u_pool = area[:, 1036:1036 + NG * 271].rearrange("p (c t) -> p c t", c=NG)
        gates = area[:, 0:CH].rearrange("p (s t) -> p s t", s=8)
        pooled = vb_pool[:, :].rearrange("p (c t) -> p c t", c=NG)
        sq = cacc[:, :, :].rearrange("p (s c) t -> p s (c t)", s=2)

        def col(j, r):
            return par[:, j, r:r + 1]
        R_GATE, R_NORM, R_CB, R_LG, R_LB, R_PS, R_MB = 44, 68, 92, 96, 100, 104, 108
        R_MW, R_MG, R_FG, R_MEMG = 0, 64, 72, 80
        PAR_ROWS = (124, 124, 88)

        def flat2(t):
            return t[:, :, :].rearrange("p a b -> p (a b)")
        e_raw = [*raw, flat2(mem_t), area, flat2(xf)]
        h_tok = q_t[:, :, :].rearrange("p (t k) n -> p t (k n)", t=TT)
        y_tok = flat2(k_t)[:, 0:D]
        before = flat2(k_t)[:, D:D + P]
        iota_slot = flat2(k_t)[:, D + P:D + 2 * P]
        vflat = vx[:, :, :, :].rearrange("p a b c -> p (a b c)")
        sel, sel_g = (vflat[:, i * T:(i + 1) * T].rearrange("p (t s) -> p t s", t=TT) for i in range(2))
        g_slot = vflat[:, 2 * T:3 * T]
        x_hi, x_lo = (flat2(t)[:, 0:D].rearrange("p (k s) -> p k s", k=KB) for t in (a_hi, a_lo))
        hid_e = [tuple(flat2(t)[:, D + i * FG:D + (i + 1) * FG].rearrange("p (k s) -> p k s", k=4) for t in (a_hi, a_lo)) for i in range(2)]
        act_e = [flat2(z_sig)[:, i * FG:(i + 1) * FG] for i in range(2)]
        rw = flat2(wif)[:, 0:KB * NE].rearrange("p (k e) -> p k e", k=KB)
        rt = flat2(u_pad)
        take = iter(range(0, 1144, 8))

        def table(n):
            first = next(take)
            for _ in range((n + 7) // 8 - 1):
                next(take)
            return rt[:, first:first + n]
        logit, cand, oh1, oh2, r_gate, r_mask, r_rank = ([table(NE) for _ in range(TT)] for _ in range(7))
        x_rank, x_mask, x_gate = ([table(XW) for _ in range(TT)] for _ in range(3))
        best, second, pick1, pick2, gap, gap_e, g1, g2 = (table(TT) for _ in range(8))
        iota8, iota8p, total, over, incl, excl, zero8 = (table(NE) for _ in range(7))
        prods = [table(NE) for _ in range(1 + 3 * TT)]
        over_oh = [table(NE) for _ in range(N_OVER)]
        ids_f = table(16)
        ids = sb("ids", [1, 16], I32)

        ps = [ctx.enter_context(nc.psum_tensor(f"ps{i}", [P, 512], F32)) for i in range(8)]

        landed = [sem(f"raw_landed{i}") for i in range(RAW)]
        par_in = sig("params_landed", 16 * 15)
        wif_in = sig("wif_landed", 16 * 2)
        vb_in = sig("v_bias_landed", 16)
        ifb_in = sig("if_bias_landed", 32)
        x_in = [sem(f"x_landed{i}") for i in range(2)]
        hi_done = sig("hi_done", N_MIX, N_FF, before=RAW)
        lo_done = sig("lo_done", N_MIX, N_FF, before=RAW)
        pe_chunk = sig("chunk_multiplied", N_MIX, N_FF, before=SPL)
        const_done = sem("constants_done")
        start_t = sem("inputs_transposed")
        start_c = sem("inputs_copied")
        par_t = sig("params_transposed", 1)
        par_c = sig("params_copied", 1)
        squared = sig("squared", 12, before=4)
        summed = sig("squares_summed", 12, before=4)
        std_done = sig("std_done", 3, before=1)
        xf_done = sig("normalised", 12, before=4)
        n_hi = sig("norm_hi", 12)
        n_lo = sig("norm_lo", 12)
        wif_split = sig("wif_split", 2)
        if_mul = sig("if_multiplied", 1)
        if_dve = sig("if_dve", 2)
        if_act = sig("if_act", 2)
        if_tr = sig("if_transposed", 1)
        gcols_done = sig("gate_columns", 1)
        pads_done = sig("pads_cleared", 1, before=1)
        qk_pre = sig("qk_biased", 8)
        qk_conv = sig("qk_convolved", 8)
        qk_done = sig("qk_done", 8)
        v_done = sig("v_done", 4)
        b_sig = sig("b_sigmoid", 2)
        u_done = sig("conv_input", 2)
        c31_done = sig("conv_done_pool", 1)
        c31_dve = sig("conv_done_dve", 1)
        pool_pre = sig("pool_input", 2)
        pool_done = sig("pooled", 1)
        pool_hi = sig("pooled_hi", 1)
        pool_lo = sig("pooled_lo", 1)
        pw_done = sig("pool_scaled", 1)
        pw_hi = sig("pool_out_hi", 1)
        pw_lo = sig("pool_out_lo", 1)
        z_done = sig("z_done", 4)
        gate_done = sig("gate_sigmoid", 12)
        gate_used = sig("gate_used", 8)
        score_mul = sig("scores_multiplied", HEADS)
        m_bcast = sig("max_broadcast", HEADS)
        dec_exp = sig("decay_exp", HEADS)
        dec_done = sig("decay_masked", HEADS)
        wdk_done = sig("decayed_scores", HEADS)
        num_mul = sig("numerators", HEADS)
        hid_done = sig("hidden_done", HEADS)
        hid_std = sig("hidden_std", 1)
        hid_nrm = sig("hidden_normalised", 1)
        hid_t = sig("hidden_transposed", 4)
        hid_gated = sig("hidden_gated", 4)
        hid_hi = sig("hidden_hi", 4)
        hid_lo = sig("hidden_lo", 4)
        ln_sum = sig("ln_sums", 1)
        ln_cent = sig("ln_centred", 1)
        ln_sq = sig("ln_squared", 1)
        ln_var = sig("ln_squares_summed", 1)
        ln_std = sig("ln_std", 1)
        ln_nrm = sig("ln_normalised", 1)
        ln_silu = sig("ln_silu", 1)
        ln_hi = sig("ln_hi", 1)
        ln_lo = sig("ln_lo", 1, before=1)
        y_done = sig("merged", 4)
        y_hi = sig("merged_hi", 4)
        y_lo = sig("merged_lo", 4)
        h_mix = sig("h_after_mixer", 4)
        mem_hi = sig("mem_hi", 8)
        mem_lo = sig("mem_lo", 8)
        xk_done = sig("xk_done", 4)
        xv_done = sig("xv_done", 4)
        xq_done = sig("xq_done", 4)
        xs_mul = sig("x_scores", HEADS)
        xmax = sig("x_max", HEADS)
        xexp = sig("x_exp", HEADS)
        xprob = sig("x_probs", HEADS)
        xp_t = sig("x_probs_transposed", HEADS)
        xp_c = sig("x_probs_copied", HEADS)
        xo_mul = sig("x_out", HEADS)
        xo_done = sig("x_out_copied", HEADS)
        xo_hi = sig("x_out_hi", HEADS)
        xo_lo = sig("x_out_lo", HEADS)
        h_att = sig("h_after_attention", 4)
        ff_silu = sig("ff_silu", 0, N_FFG)
        ff_mul = sig("ff_gated", 0, N_FFG)
        ff_hi = sig("ff_hi", 0, N_FFG)
        ff_lo = sig("ff_lo", 0, N_FFG)
        h_ff = sig("h_after_ff", 0, 4, before=4)
        def esig(name, per_block, before=0):
            e = Signal(ctx, nc, name, per_block, 0, before)
            return e
        e_landed = [sem(f"e_landed{i}") for i in range(ERAW)]
        e_hi, e_lo = esig("e_hi", N_EXP), esig("e_lo", N_EXP, ERAW)
        e_pe = esig("e_multiplied", N_EXP, SPL)
        free = sem("e_chunk_free")
        rw_in = sem("router_landed")
        e_const = sem("e_constants")
        logits_mul, tok_t, tok_c = sem("logits"), sem("stream_transposed"), sem("stream_copied")
        r_gap, r_exp, mask_done, rank_mul, ids_done = sem("gate_gap"), sem("gate_exp"), sem("mask_done"), sem("rank_sums"), sem("ids_done")
        sel_done = esig("selected", 1)
        gathered, x_hi_done, x_lo_done = esig("gathered", 2), esig("x_hi", 2), esig("x_lo", 2)
        e_silu, e_gated, e_turned = esig("e_silu", NGE), esig("e_gated", NGE), esig("e_turned", NGE)
        e_hid_hi, e_hid_lo = esig("e_hidden_hi", NGE), esig("e_hidden_lo", NGE)
        g_turned, g_copied = esig("g_turned", 1), esig("g_copied", 1)
        y_copied = esig("y_copied", 1, 1)
        spread = esig("spread", 4)
        h_added = esig("h_added", 4, 4)
        settled = sem("experts_settled")
        f_sq, f_sum, f_std, f_x, f_t = sem("f_squared"), sem("f_summed"), sem("f_std"), sem("f_normalised"), sem("f_turned")
        dve_chain, act_chain, pool_chain = sem("dve_chain"), sem("act_chain"), sem("pool_chain")
        out_ready, out_sem = sem("out_ready"), sem("out_stored")

        block = ctx.enter_context(nc.Block())

        def at_layer(a, layer):
            return a[bass.ds(layer, 1)]

        def chunk_source(layer, c):
            def cols(name, c0):
                return at_layer(w[name], layer)[:, :, c0:c0 + T].rearrange("o (k p) n -> p (o k) n", p=P)

            def half(name, i):
                return at_layer(w[name], layer)[:, :, i * 512:(i + 1) * 512].rearrange("o (k p) n -> p (o k) n", p=P)
            if c < QK0:
                i = c - AB0
                return cols("w_in", (C_A if i % 2 else C_B) + (i // 2) * T)
            if c < V0:
                return cols("w_in", C_Q + (c - QK0) * T)
            if c < PU0:
                return cols("w_in", C_V + (c - V0) * T)
            if c < Z0:
                return cols("w_in", C_POOL + (c - PU0) * T)
            if c < PW:
                return cols("w_in", C_Z + (c - Z0) * T)
            if c == PW:
                return at_layer(w["pool_w"], layer).rearrange("o g c d -> c (o g) d")
            if c < WP0:
                return cols("w_in", C_G + D + (c - GB0) * T)
            if c < GA0:
                return half("w_pool_out", c - WP0)
            if c < WC0:
                return cols("w_in", C_G + (c - GA0) * T)
            if c < GC0:
                return half("w_conv_out", c - WC0)
            if c < WO0:
                i = c - GC0
                return cols("w_mlstm_out", (i // 2) * T) if i % 2 else cols("w_in", C_G + 2 * D + (i // 2) * T)
            if XV1 <= c < XO0:
                return cols("xa_wv", (c - XV1 + 1) * T)
            for first, name in ((XO0, "xa_wo"), (XQ0, "xa_wq"), (XV0, "xa_wv"), (XK0, "xa_wk"), (WO0, "w_out")):
                if c >= first:
                    return cols(name, (c - first) * T)

        def ff_source(j):
            what, g, i = FF_SEQ[j]
            if what == "up":
                return w[("ffn_w1", "ffn_w3")[i]][0, :, g * T:(g + 1) * T].rearrange("(k p) n -> p k n", p=P)
            return w["ffn_w2"][0, g * T:(g + 1) * T, :].rearrange("(k p) n -> p k n", p=P)

        def shaped(t, src):
            k, n = src.shape[1], src.shape[2]
            return t[:, 0:k * n].rearrange("p (k n) -> p k n", k=k)

        def kn(t, k):
            return t[:, :].rearrange("p (k n) -> p k n", k=k)

        def chunk_len(c):
            return 512 if c == PW else CH

        @block.sync
        def _(sp):
            sp.dma_start(q_t[:, :, :].rearrange("p (t k) n -> p t (k n)", t=TT), w["x"][0].rearrange("(t p) d -> p t d", p=P)).then_inc(x_in[0], 16)
            sp.dma_start(k_t[:, :, :].rearrange("p (t k) n -> p t (k n)", t=TT), w["mem"][0].rearrange("(t p) d -> p t d", p=P)).then_inc(x_in[1], 16)

            def params(layer):
                def r(name, tile, row, n, c0=0):
                    a = at_layer(w[name], layer)[:, c0:c0 + n * P].rearrange("o (r p) -> (o r) p", p=P)
                    sp.dma_start(prow[row:row + n, tile, :], a).then_inc(par_in.sem, 16)
                r("b_in", 0, 0, 44)
                r("b_in", 0, R_GATE, 24, C_G)
                r("norm_mix_g", 0, R_NORM, 8)
                r("norm_xattn_g", 0, R_NORM + 8, 8)
                r("norm_ffn_g", 0, R_NORM + 16, 8)
                r("conv_dw_b", 0, R_CB, 4)
                r("conv_ln_g", 0, R_LG, 4)
                r("conv_ln_b", 0, R_LB, 4)
                r("pool_scale", 0, R_PS, 4)
                r("mlstm_conv_b", 0, R_MB, 16)
                sp.dma_start(prow[0:124, 1, :], at_layer(w["conv_dw_w"], layer).rearrange("o k (c p) -> (o k c) p", p=P)).then_inc(par_in.sem, 16)
                sp.dma_start(prow[0:64, 2, :], at_layer(w["mlstm_conv_w"], layer).rearrange("o k (c p) -> (o k c) p", p=P)).then_inc(par_in.sem, 16)
                r("mlstm_norm_g", 2, R_MG, 8)
                for row, name in ((R_FG, "final_norm_g"), (R_MEMG, "mem_norm_g")):
                    sp.dma_start(prow[row:row + 8, 2, :], w[name].rearrange("(r p) -> r p", p=P)).then_inc(par_in.sem, 16)
                sp.dma_start(vb_pool[:, :], at_layer(w["b_in"], layer)[:, C_V:C_V + D].broadcast_to([P, D])).then_inc(vb_in.sem, 16)
                for lane, c0 in ((0, C_I), (32, C_F)):
                    src = at_layer(w["b_in"], layer)[:, c0:c0 + HEADS].rearrange("o h -> h o")
                    sp.dma_start(if_bias[lane:lane + HEADS, :], src).then_inc(ifb_in.sem, 16)
                    src = at_layer(w["w_in"], layer)[:, :, c0:c0 + HEADS].rearrange("o (k p) n -> p (o k) n", p=P)
                    sp.dma_start(wif[:, :, lane:lane + HEADS], src).then_inc(wif_in.sem, 16)

            def load(layer, c, src):
                sp.wait_ge(hi_done.sem, hi_done.at(layer, c + 1 - RAW))
                sp.wait_ge(lo_done.sem, lo_done.at(layer, c + 1 - RAW))
                sp.dma_start(shaped(raw[c % RAW], src), src).then_inc(landed[c % RAW], 16)

            sp.wait_ge(const_done, CONSTS)
            params(0)
            for layer in range(DEPTH):
                for c in range(N_MIX):
                    load(layer, c, chunk_source(layer, c))
                if layer == 0:
                    sp.wait_ge(par_t.sem, par_t.at(layer, 1))
                    sp.wait_ge(wif_split.sem, wif_split.at(layer, 2))
                    sp.wait_ge(pw_lo.sem, pw_lo.at(layer, 1))
                    sp.wait_ge(if_dve.sem, if_dve.at(layer, 2))
                    params(layer + 1)
                    for j in range(N_FF):
                        load(layer, N_MIX + j, ff_source(j))
            sp.wait_ge(wif_split.sem, wif_split.moe)
            sp.dma_start(rw, w["router_w"][0].rearrange("(k p) e -> p k e", p=P)).then_inc(rw_in, 16)

            def expert_source(e, m):
                kind, g, i = ESEQ[m]
                a = w["moe_" + kind][0, bass.ds(e, 1)]
                if kind == "w2":
                    r0 = g * FG + i * 2 * P
                    return a[:, r0:r0 + 2 * P, :].rearrange("o (k p) n -> p (o k) n", p=P)
                return a[:, i * 4 * P:(i + 1) * 4 * P, g * FG:(g + 1) * FG].rearrange("o (k p) n -> p (o k) n", p=P)

            def expert_load(b, m, e):
                sp.wait_ge(e_lo.sem, e_lo.at(b, m + 1 - ERAW))
                sp.sem_inc(free, 1)
                sp.wait_ge(lo_done.sem, lo_done.moe + min(m + 1 - RAW, 0))
                if m == 3:
                    sp.wait_ge(mem_lo.sem, mem_lo.moe)
                elif m == 4:
                    sp.wait_ge(pads_done.sem, pads_done.moe)
                elif m == 5:
                    sp.wait_ge(tok_t, 4)
                    sp.wait_ge(logits_mul, 1)
                    sp.wait_ge(n_lo.sem, n_lo.moe)
                src = expert_source(e, m)
                sp.dma_start(shaped(e_raw[m % ERAW], src), src).then_inc(e_landed[m % ERAW], 16)

            def expert_block(b, e):
                for m in range(SPL, N_EXP):
                    expert_load(b, m, e)
                sp.wait_ge(ids_done, 1)
                nxt = sp.value_load(ids[0:1, bass.ds(b + 1, 1)], min_val=0, max_val=NE - 1)
                for m in range(SPL):
                    expert_load(b + 1, m, nxt)
            sp.sem_inc(e_lo.sem, ERAW)
            for m in range(SPL):
                expert_load(0, m, 0)
            with sp.Fori(0, NE) as b:
                expert_block(b, b)
            more = sp.value_load(ids[0:1, NBLK + 1:NBLK + 2], min_val=NE, max_val=NBLK)
            with sp.Fori(NE, NBLK) as b:
                with sp.If(b < more):
                    expert_block(b, sp.value_load(ids[0:1, bass.ds(b, 1)], min_val=0, max_val=NE - 1))
            sp.wait_ge(out_ready, 4)
            for t in range(TT):
                sp.dma_start(out[0, t * P:(t + 1) * P, :], q_t[:, 4 * t:4 * t + 4, :].rearrange("p k n -> p (k n)")).then_inc(out_sem, 16)
            sp.wait_ge(out_sem, 32)

        @block.gpsimd
        def _(pool):
            ch = Chain(pool, pool_chain, 0)
            ch.did(pool.memset(ident[:, :], 0.0))
            ch.did(pool.memset(selh[:, :, :], 0.0))
            for g, win in enumerate(POOL_WINDOWS):
                last = ch.did(pool.memset(rcnt[:, g, :], 1.0 / win))
            ch.need(last)
            for g, win in enumerate(POOL_WINDOWS):
                for t in range(win - 1):
                    last = ch.did(pool.memset(rcnt[:, g, t:t + 1], 1.0 / (t + 1)))
            ch.need(last)
            pool.affine_select(out=ident[:, :], in_=ident[:, :], compare_op=ALU.not_equal, fill=1.0, base=0,
                               pattern=[[-1, P]], channel_multiplier=1).then_inc(const_done, 1)
            pool.affine_select(out=selh[:, :, :], in_=selh[:, :, :], compare_op=ALU.not_equal, fill=1.0, base=0,
                               pattern=[[-1, HEADS], [0, P]], channel_multiplier=1).then_inc(const_done, 1)
            pool.memset(ones[:, :], 1.0).then_inc(const_done, 1)
            pool.memset(eps[:, :], EPS).then_inc(const_done, 1)
            pool.memset(wif[:, :, :], 0.0).then_inc(const_done, 1)
            pool.memset(zrow[:, :], 0.0).then_inc(const_done, 1)
            pool.memset(u_pad[:, :, 0:CONV_K - 1], 0.0).then_inc(const_done, 1)
            pool.memset(vx[:, :, :, DH:DH + 1], 1.0).then_inc(const_done, 1)
            pool.memset(pre[:, :, 0:MCONV_K - 1], 0.0).then_inc(const_done, 1)
            pool.memset(u_pool[:, :, 0:15], 0.0).then_inc(pads_done.sem, 1)

            def mixer(layer):
                pool.wait_ge(u_done.sem, u_done.at(layer, 1))
                pool.wait_ge(par_c.sem, par_c.at(layer, 1))
                pool.wait_ge(n_lo.sem, n_lo.at(layer, 4))
                pool.wait_ge(ln_lo.sem, ln_lo.at(layer, 0))
                for c in range(2):
                    last = ch.did(pool.tensor_scalar(c31[:, c, :], u_pad[:, c, 0:T], col(1, c), col(0, R_CB + c), ALU.mult, ALU.add))
                total = c31[:, 0:2, :]
                for k in range(1, CONV_K):
                    tap = par[:, 1, k * CB:k * CB + 2].rearrange("p (c o) -> p c o", o=1).broadcast_to([P, 2, T])
                    ch.need(last)
                    ch.link(pool.tensor_tensor(taps[:, k % 2], u_pad[:, 0:2, k:k + T], tap, ALU.mult))
                    ins = pool.tensor_tensor(total, total, taps[:, k % 2], ALU.add)
                    if k == CONV_K - 1:
                        ins.then_inc(c31_done.sem, 1)
                    else:
                        last = ch.did(ins)
                for hd in range(HEADS):
                    pool.wait_ge(dec_exp.sem, dec_exp.at(layer, hd + 1))
                    d = dec[:, hd % 2, :].rearrange("p (b t) -> p b t", b=3)[:, 0:3:2, :]
                    pool.affine_select(out=d, in_=d, compare_op=ALU.is_ge, fill=0.0, base=0,
                                       pattern=[[0, 2], [1, P]], channel_multiplier=-1).then_inc(dec_done.sem, 1)
                pool.wait_ge(y_done.sem, y_done.at(layer, 4))
                ch.did(pool.memset(pre[:, :, 0:MCONV_K - 1], 0.0))
                ch.need(ch.n)
                pool.memset(u_pool[:, :, 0:15], 0.0).then_inc(pads_done.sem, 1)

            for layer in range(DEPTH):
                mixer(layer)
            pool.wait_ge(xs_mul.sem, xs_mul.moe)
            ch.link(pool.memset(before, 1.0))
            pool.affine_select(out=before, in_=before, compare_op=ALU.is_gt, fill=0.0, base=0,
                               pattern=[[1, P]], channel_multiplier=-1).then_inc(e_const, 1)
            pool.iota(iota_slot, pattern=[[1, P]], base=0, channel_multiplier=0, allow_small_or_imprecise_dtypes=True).then_inc(e_const, 1)
            pool.iota(iota8, pattern=[[1, NE]], base=0, channel_multiplier=0, allow_small_or_imprecise_dtypes=True).then_inc(e_const, 1)
            pool.iota(iota8p, pattern=[[1, NE]], base=NE, channel_multiplier=0, allow_small_or_imprecise_dtypes=True).then_inc(e_const, 1)
            pool.memset(zero8, 0.0).then_inc(e_const, 1)
            for t in (*x_rank, *x_mask, *x_gate, ids_f):
                pool.memset(t, 0.0).then_inc(e_const, 1)

        GATE_NO = {c: n for n, c in enumerate([*range(GB0, WP0), *range(GA0, WC0), *range(GC0, WO0, 2)])}

        def bank(key, part=0):
            return ps[PLAN[key][part][0]]

        def read_by(key, part):
            if key == "hidden_t":
                return hid_gated, part + 1
            c = key[1]
            if c < QK0:
                return (u_done if (c - AB0) % 2 else b_sig), (c - AB0) // 2 + 1
            if c < V0:
                return qk_pre, c - QK0 + 1
            if c < PU0:
                return v_done, c - V0 + 1
            if c < Z0:
                return pool_pre, c - PU0 + 1
            if c < PW:
                return z_done, c - Z0 + 1
            if c == PW:
                return pw_done, 1
            if c in GATE_NO:
                return gate_done, GATE_NO[c] + 1
            if WP0 <= c < GA0:
                return gate_used, 2 * (c - WP0) + part + 1
            if WC0 <= c < GC0:
                return gate_used, 4 + 2 * (c - WC0) + part + 1
            if c < WO0:
                return y_done, (c - GC0) // 2 + 1
            for first, s, n in ((XO0, h_att, 0), (XV1, xv_done, 1), (XQ0, xq_done, 0), (XV0, xv_done, 0), (XK0, xk_done, 0), (WO0, h_mix, 0)):
                if c >= first:
                    return s, c - first + n + 1

        def flat(a):
            return a.rearrange("p c t -> p (c t)")

        def as_f32(a):
            return a.bitcast(F32)

        DEN, SS, STD, RST, TMP, NMAX, XSUM, XREC = 0, 8, 16, 24, 32, 48, 50, 52

        @block.scalar
        def _(act):
            ch = Chain(act, act_chain, 0)

            def split(layer, c, n=CH):
                act.wait_ge(landed[c % RAW], 16 * (layer * (N_LAYER // RAW) + c // RAW + 1))
                act.wait_ge(pe_chunk.sem, pe_chunk.at(layer, c + 1 - SPL))
                act.activation(w_hi[c % SPL][:, 0:n], raw[c % RAW][:, 0:n], ACT.Copy).then_inc(hi_done.sem, 1)

            def e_split(b, m):
                act.wait_ge(e_landed[m % ERAW], 16 * (b * (N_EXP // ERAW) + (m // ERAW + 1)))
                act.wait_ge(e_pe.sem, e_pe.at(b, m + 1 - SPL))
                if m < SPL:
                    act.wait_ge(pe_chunk.sem, pe_chunk.moe + m + 1 - SPL)
                act.activation(w_hi[m % SPL][:, :], e_raw[m % ERAW][:, 0:CH], ACT.Copy).then_inc(e_hi.sem, 1)

            def square(layer, n, j, src=h):
                act.wait_ge(summed.sem, summed.at(layer, 4 * n + j - 1))
                act.activation(sq[:, j % 2, :], flat(src[:, 2 * j:2 * j + 2, :]), ACT.Square).then_inc(squared.sem, 1)

            def std(layer, n):
                act.wait_ge(summed.sem, summed.at(layer, 4 * n + 4))
                act.activation(rstd[:, 0, :], ps[4][:, 0:T], ACT.Sqrt, bias=eps[:, 0:1], scale=1.0 / D).then_inc(std_done.sem, 1)

            def norm_hi(layer, n, dst):
                for j in range(4):
                    act.wait_ge(xf_done.sem, xf_done.at(layer, 4 * n + j + 1))
                    act.activation(dst[:, 2 * j:2 * j + 2, :], xf[:, 2 * j:2 * j + 2, :], ACT.Copy).then_inc(n_hi.sem, 1)

            def multiplied(layer, j):
                act.wait_ge(pe_chunk.sem, pe_chunk.at(layer, j + 1))

            def biased(layer, j, dst, func, row, done):
                multiplied(layer, j)
                for i in range(2):
                    ins = act.activation(dst(i), bank(("chunk", j))[:, i * HALF:(i + 1) * HALF], func, bias=col(0, row + i))
                ins.then_inc(done.sem, 1)

            def qk_input(layer, j):
                act.wait_ge(pads_done.sem, pads_done.at(layer, 0))
                if j >= 2:
                    act.wait_ge(qk_conv.sem, qk_conv.at(layer, j - 1))
                biased(layer, QK0 + j, lambda i: pre[:, 2 * (j % 2) + i, 3:3 + T], ACT.Identity, C_Q // P + 2 * j, qk_pre)

            def qk_silu(layer, j):
                act.wait_ge(qk_conv.sem, qk_conv.at(layer, j + 1))
                dst = (q_t if j < 4 else k_t)[:, 2 * (j % 4):2 * (j % 4) + 2, :]
                s = 2 * (j % 2)
                act.activation(dst, cacc[:, s:s + 2, :], ACT.Silu).then_inc(qk_done.sem, 1)

            def forget_rows(layer):
                act.wait_ge(if_dve.sem, if_dve.at(layer, 1))
                ch.link(act.activation(rows[:, 2, :], rows[:, 1, :], ACT.Abs))
                ch.link(act.activation(rows[:, 3, :], rows[:, 2, :], ACT.Exp, scale=-1.0))
                act.activation(rows[:, 2, :], rows[:, 3, :], ACT.Ln, bias=1.0).then_inc(if_act.sem, 1)

            def bound_row(layer):
                act.wait_ge(if_dve.sem, if_dve.at(layer, 2))
                act.activation(rows[:, 2, :], rows[:, 3, :], ACT.Exp).then_inc(if_act.sem, 1)

            def decay(layer, hd):
                act.wait_ge(m_bcast.sem, m_bcast.at(layer, hd + 1))
                act.wait_ge(gcols_done.sem, gcols_done.at(layer, 1))
                if hd >= 2:
                    act.wait_ge(wdk_done.sem, wdk_done.at(layer, hd - 1))
                act.activation(dec[:, hd % 2, 0:T], ps[4][:, 0:T], ACT.Exp, bias=gcols[:, hd:hd + 1], scale=-1.0)
                act.activation(dec[:, hd % 2, T:3 * P], ps[4][:, P:T], ACT.Exp, bias=gcols[:, 4 + hd:5 + hd], scale=-1.0).then_inc(dec_exp.sem, 1)

            def hidden_squares(layer, hd):
                act.wait_ge(hid_done.sem, hid_done.at(layer, hd + 1))
                for tt in range(TT):
                    n = SS + 2 * hd + tt
                    ch.link(act.activation(sgb[:, 0, :], q_t[:, 2 * hd + tt, :], ACT.Square, accum_out=small[:, n:n + 1]))

            def gate(layer, j):
                n = GATE_NO[j]
                if n >= 4:
                    act.wait_ge(gate_used.sem, gate_used.at(layer, n - 3))
                else:
                    act.wait_ge(pool_done.sem, pool_done.at(layer, 1))
                branch, q = (1, 0, 2)[n // 4], n % 4
                biased(layer, j, lambda i: gates[:, 2 * q + i, :], ACT.Sigmoid, R_GATE + KB * branch + 2 * q, gate_done)

            def merged_hi(layer, q):
                act.wait_ge(pe_chunk.sem, pe_chunk.at(layer, WO0 - 1))
                act.wait_ge(y_done.sem, y_done.at(layer, q + 1))
                act.activation(a_hi[:, 2 * q:2 * q + 2, :], xf[:, 2 * q:2 * q + 2, :], ACT.Copy).then_inc(y_hi.sem, 1)

            def x_exp(layer, hd):
                act.wait_ge(xmax.sem, xmax.at(layer, hd + 1))
                if hd >= 2:
                    act.wait_ge(xp_t.sem, xp_t.at(layer, hd - 1))
                for tt in range(TT):
                    ins = act.activation(z_sig[:, 2 * (hd % 2) + tt, :], ps[4 + hd % 2][:, tt * T:(tt + 1) * T], ACT.Exp,
                                         bias=xcols[:, 0, hd, tt:tt + 1], scale=DH ** -0.5, accum_out=xcols[:, 1, hd, tt:tt + 1])
                ins.then_inc(xexp.sem, 1)

            def x_copy(layer, hd):
                act.wait_ge(xp_t.sem, xp_t.at(layer, hd + 1))
                if hd >= 2:
                    act.wait_ge(xo_mul.sem, xo_mul.at(layer, hd - 1))
                s = 4 + 2 * (hd % 2)
                act.activation(flat(z_sig[:, s:s + 2, :]), ps[6][:, :], ACT.Copy).then_inc(xp_c.sem, 1)

            def x_out_hi(layer, hd):
                act.wait_ge(xo_done.sem, xo_done.at(layer, hd + 1))
                act.activation(a_hi[:, 2 * hd:2 * hd + 2, :], xf[:, 2 * hd:2 * hd + 2, :], ACT.Copy).then_inc(xo_hi.sem, 1)

            def post(layer, j):
                if QK0 <= j < V0:
                    qk_input(layer, j - QK0)
                elif j < QK0 and (j - AB0) % 2 == 0:
                    i = (j - AB0) // 2
                    if i:
                        act.wait_ge(u_done.sem, u_done.at(layer, i))
                    biased(layer, j, lambda n: sgb[:, n, :], ACT.Sigmoid, C_B // P + 2 * i, b_sig)
                elif PU0 <= j < Z0:
                    i = j - PU0
                    biased(layer, j, lambda n: u_pool[:, 2 * i + n, 15:15 + T], ACT.Identity, C_POOL // P + 2 * i, pool_pre)
                elif Z0 <= j < PW:
                    i = j - Z0
                    biased(layer, j, lambda n: z_sig[:, 2 * i + n, :], ACT.Sigmoid, C_Z // P + 2 * i, z_done)
                elif j in GATE_NO:
                    gate(layer, j)
                elif XK0 <= j < XV0:
                    i = j - XK0
                    multiplied(layer, j)
                    act.activation(flat(k_t[:, 2 * i:2 * i + 2, :]), bank(("chunk", j))[:, :], ACT.Copy).then_inc(xk_done.sem, 1)
                if j == QK0:
                    forget_rows(layer)
                if QK0 < j <= V0:
                    qk_silu(layer, j - QK0 - 1)
                if j == QK0 + 2:
                    bound_row(layer)
                if j == Z0 + 1:
                    act.wait_ge(pool_done.sem, pool_done.at(layer, 1))
                    act.activation(b_hi[:, 4:8, :], pooled, ACT.Copy).then_inc(pool_hi.sem, 1)
                if j == PW:
                    act.wait_ge(pw_done.sem, pw_done.at(layer, 1))
                    act.activation(b_hi[:, 0:4, :], pooled, ACT.Copy).then_inc(pw_hi.sem, 1)
                if j in SCORES:
                    decay(layer, SCORES.index(j))
                if j - 2 in SCORES:
                    hidden_squares(layer, SCORES.index(j - 2))
                if j == SCORES[-1] + 3:
                    act.activation(small[:, STD:STD + 8], small[:, SS:SS + 8], ACT.Sqrt, bias=eps[:, 0:1], scale=1.0 / DH).then_inc(hid_std.sem, 1)
                if j == LN_MEAN:
                    act.wait_ge(ln_cent.sem, ln_cent.at(layer, 1))
                    act.activation(cacc[:, :, :], c31[:, :, :], ACT.Square).then_inc(ln_sq.sem, 1)
                if j == LN_VAR:
                    act.wait_ge(ln_var.sem, ln_var.at(layer, 1))
                    act.activation(rstd[:, 0, :], ps[5][:, 0:T], ACT.Sqrt, bias=eps[:, 0:1], scale=1.0 / CONV_W).then_inc(ln_std.sem, 1)
                    act.wait_ge(ln_nrm.sem, ln_nrm.at(layer, 1))
                    for c in range(CB):
                        ins = act.activation(c31[:, c, :], c31[:, c, :], ACT.Silu, bias=col(0, R_LB + c))
                    ins.then_inc(ln_silu.sem, 1)
                    act.wait_ge(ln_silu.sem, ln_silu.at(layer, 1))
                    act.activation(b_hi[:, 4:8, :], c31[:, :, :], ACT.Copy).then_inc(ln_hi.sem, 1)
                if j == GC0 - 1:
                    multiplied(layer, j)
                    for i in range(4):
                        act.wait_ge(hid_gated.sem, hid_gated.at(layer, i + 1))
                        act.activation(b_hi[:, 2 * i:2 * i + 2, :], k_t[:, 2 * i:2 * i + 2, :], ACT.Copy).then_inc(hid_hi.sem, 1)
                if j == WO0 - 2:
                    for q in range(3):
                        merged_hi(layer, q)
                if j == WO0 - 1:
                    merged_hi(layer, 3)
                if j == WO0:
                    for k in range(KB):
                        act.activation(b_hi[:, k, :], mem_t[:, k, :], ACT.Copy, scale=col(2, R_MEMG + k)).then_inc(mem_hi.sem, 1)
                if WO0 <= j < XK0:
                    act.wait_ge(h_mix.sem, h_mix.at(layer, j - WO0 + 1))
                    square(layer, 1, j - WO0)
                if j == XK0 + 1:
                    std(layer, 1)
                    norm_hi(layer, 1, a_hi)
                if XQ0 + 1 <= j < XQ0 + 1 + HEADS:
                    x_exp(layer, j - XQ0 - 1)
                if XQ0 + 2 <= j < XQ0 + 2 + HEADS:
                    x_copy(layer, j - XQ0 - 2)
                for hd in X_OUT_AFTER.get(j, ()):
                    x_out_hi(layer, hd)
                if XO0 <= j < N_MIX:
                    act.wait_ge(h_att.sem, h_att.at(layer, j - XO0 + 1))
                    square(layer, 2, j - XO0)

            def ahead(layer, m):
                if layer == 0:
                    split(layer, N_MIX + m)
                else:
                    e_split(0, m)

            def mixer(layer):
                if layer == 0:
                    split(layer, 0)
                for j in range(4):
                    act.wait_ge(h_ff.sem, h_ff.at(layer, j - 3))
                    square(layer, 0, j)
                std(layer, 0)
                norm_hi(layer, 0, a_hi)
                if layer:
                    split(layer, SPL - 1)
                act.wait_ge(wif_in.sem, wif_in.at(layer, 32))
                act.activation(wif_hi[:, :, :], wif[:, :, :], ACT.Copy).then_inc(wif_split.sem, 1)
                for c in range(SPL if layer else 1, N_MIX + SPL):
                    if c < N_MIX:
                        split(layer, c, chunk_len(c))
                    if c >= SPL:
                        post(layer, c - SPL)
                    if N_MIX <= c < N_MIX + SPL - 1:
                        ahead(layer, c - N_MIX)
                std(layer, 2)
                norm_hi(layer, 2, b_hi)
                ahead(layer, SPL - 1)

            def dense(layer):
                def silu(g):
                    if g >= 2:
                        act.wait_ge(ff_lo.sem, ff_lo.at(layer, g - 1))
                    act.wait_ge(pe_chunk.sem, pe_chunk.at(layer, N_MIX + FF_SEQ.index(("up", g, 0)) + 1))
                    s = 2 * (g % 2)
                    act.activation(flat(z_sig[:, s:s + 2, :]), ps[(2 * g) % 4][:, :], ACT.Silu).then_inc(ff_silu.sem, 1)

                def gated_hi(g):
                    act.wait_ge(ff_mul.sem, ff_mul.at(layer, g + 1))
                    s, d = 2 * (g % 2), 2 * (g % 4)
                    act.activation(a_hi[:, d:d + 2, :], z_sig[:, s:s + 2, :], ACT.Copy).then_inc(ff_hi.sem, 1)
                for c in range(SPL, N_FF + SPL):
                    if c < N_FF:
                        split(layer, N_MIX + c)
                    what, g, i = FF_SEQ[c - SPL]
                    if what == "up":
                        silu(g) if i == 0 else gated_hi(g)
                    if N_FF <= c < N_FF + SPL - 1:
                        split(layer + 1, c - N_FF)

            act.wait_ge(const_done, CONSTS)
            for j in range(4):
                act.wait_ge(start_c, j + 1)
                if j >= 2:
                    act.wait_ge(summed.sem, j - 1)
                act.activation(sq[:, j % 2, :], flat(mem_t[:, 2 * j:2 * j + 2, :]), ACT.Square).then_inc(squared.sem, 1)
            act.wait_ge(summed.sem, 4)
            act.activation(rstd[:, 0, :], ps[4][:, 0:T], ACT.Sqrt, bias=eps[:, 0:1], scale=1.0 / D).then_inc(std_done.sem, 1)
            act.sem_inc(hi_done.sem, RAW)
            for layer in range(DEPTH):
                mixer(layer)
                if layer == 0:
                    dense(layer)
            def gather_hi(b):
                for i in range(2):
                    act.wait_ge(gathered.sem, gathered.at(b, i + 1))
                    act.activation(x_hi[:, 4 * i:4 * i + 4, :].rearrange("p k s -> p (k s)"), ps[7 - i][:, :], ACT.Copy).then_inc(x_hi_done.sem, 1)

            def e_post(b, m):
                kind, g, i = ESEQ[m]
                act.wait_ge(e_pe.sem, e_pe.at(b, m + 1))
                if kind == "w1" and i == 1:
                    if g >= 2:
                        act.wait_ge(e_turned.sem, e_turned.at(b, g - 1))
                    act.activation(act_e[g % 2], ps[(2 * g) % 4][:, :], ACT.Silu).then_inc(e_silu.sem, 1)
                turned = {E_AT["w1", n + 1, 1]: n for n in range(NGE - 1)} | {E_AT["w2", NGE - 2, 1]: NGE - 1}
                if m in turned:
                    n = turned[m]
                    act.wait_ge(e_turned.sem, e_turned.at(b, n + 1))
                    act.activation(hid_e[n % 2][0].rearrange("p k s -> p (k s)"), ps[6][:, :], ACT.Copy).then_inc(e_hid_hi.sem, 1)
                if (kind, g, i) == ("w3", 0, 1):
                    act.wait_ge(g_turned.sem, g_turned.at(b, 1))
                    act.activation(g_slot, ps[7][:, 0:T], ACT.Copy).then_inc(g_copied.sem, 1)
                if m == E_AT["w2", NGE - 2, 1]:
                    gather_hi(b + 1)
                if m == N_EXP - 1:
                    act.activation(y_tok[:, 0:512], ps[4][:, :], ACT.Copy)
                    act.activation(y_tok[:, 512:D], ps[5][:, :], ACT.Copy).then_inc(y_copied.sem, 1)

            def e_block(b):
                for t in range(SPL, N_EXP + SPL):
                    if t < N_EXP:
                        e_split(b, t)
                    e_post(b, t - SPL)
                    if t >= N_EXP:
                        e_split(b + 1, t - N_EXP)

            for i in range(4):
                act.wait_ge(tok_t, i + 1)
                act.activation(h_tok[:, i // 2, (i % 2) * 512:(i % 2 + 1) * 512], ps[i][:, :], ACT.Copy).then_inc(tok_c, 1)
            act.wait_ge(r_gap, 1)
            act.activation(gap_e, gap, ACT.Exp).then_inc(r_exp, 1)
            gather_hi(0)
            act.sem_inc(y_copied.sem, 1)
            with act.Fori(0, NE) as b:
                e_block(b)
            act.wait_ge(ids_done, 1)
            more = act.value_load(ids[0:1, NBLK + 1:NBLK + 2], min_val=NE, max_val=NBLK)
            with act.Fori(NE, NBLK) as b:
                with act.If(b < more):
                    e_block(b)
            act.drain().then_inc(settled, 1)
            act.wait_ge(settled, 3)
            for j in range(4):
                if j >= 2:
                    act.wait_ge(f_sum, j - 1)
                act.activation(sq[:, j % 2, :], flat(h[:, 2 * j:2 * j + 2, :]), ACT.Square).then_inc(f_sq, 1)
            act.wait_ge(f_sum, 4)
            act.activation(rstd[:, 0, :], ps[4][:, 0:T], ACT.Sqrt, bias=eps[:, 0:1], scale=1.0 / D).then_inc(f_std, 1)
            for i in range(4):
                act.wait_ge(f_t, i + 1)
                act.activation(h_tok[:, i // 2, (i % 2) * 512:(i % 2 + 1) * 512], ps[i][:, :], ACT.Copy).then_inc(out_ready, 1)

        @block.vector
        def _(dve):
            ch = Chain(dve, dve_chain, 0)

            def lo(dst, whole, hi):
                return dve.tensor_tensor(dst, whole, as_f32(hi), ALU.subtract)

            def split(layer, c, n=CH):
                dve.wait_ge(hi_done.sem, hi_done.at(layer, c + 1))
                lo(w_lo[c % SPL][:, 0:n], raw[c % RAW][:, 0:n], w_hi[c % SPL][:, 0:n]).then_inc(lo_done.sem, 1)

            def multiplied(layer, j):
                dve.wait_ge(pe_chunk.sem, pe_chunk.at(layer, j + 1))

            def e_split(b, m):
                dve.wait_ge(e_hi.sem, e_hi.at(b, m + 1))
                lo(w_lo[m % SPL][:, :], e_raw[m % ERAW][:, 0:CH], w_hi[m % SPL][:, :]).then_inc(e_lo.sem, 1)

            def norm(layer, n, g_row, hi, lo_t):
                dve.wait_ge(std_done.sem, std_done.at(layer, n + 1))
                ch.link(dve.reciprocal(rstd[:, 1, :], rstd[:, 0, :]))

                def low(j):
                    dve.wait_ge(n_hi.sem, n_hi.at(layer, 4 * n + j + 1))
                    lo(lo_t[:, 2 * j:2 * j + 2, :], xf[:, 2 * j:2 * j + 2, :], hi[:, 2 * j:2 * j + 2, :]).then_inc(n_lo.sem, 1)
                for j in range(4):
                    for k in (2 * j, 2 * j + 1):
                        ins = dve.scalar_tensor_tensor(xf[:, k, :], h[:, k, :], col(0, g_row + k), rstd[:, 1, :], ALU.mult, ALU.mult)
                    ins.then_inc(xf_done.sem, 1)
                    if j:
                        low(j - 1)
                low(3)

            def gate_scans(layer):
                dve.wait_ge(if_act.sem, if_act.at(layer, 1))
                ch.link(dve.scalar_tensor_tensor(rows[:, 1, :], rows[:, 1, :], 0.0, rows[:, 2, :], ALU.min, ALU.subtract))
                ch.link(dve.tensor_tensor_scan(rows[:, 3, :], zrow[:, :], rows[:, 1, :], 0.0, ALU.add, ALU.add))
                ch.link(dve.tensor_tensor(rows[:, 0, :], rows[:, 0, :], rows[:, 3, :], ALU.subtract))
                ch.link(dve.tensor_tensor_scan(m_row[:, :], zrow[:, :], rows[:, 0, :], 0.0, ALU.add, ALU.max))
                dve.scalar_tensor_tensor(rows[:, 3, :], rows[:, 3, :], -1.0, m_row[:, :], ALU.mult, ALU.subtract).then_inc(if_dve.sem, 1)

            def conv4(layer, j):
                dve.wait_ge(qk_pre.sem, qk_pre.at(layer, j + 1))
                if j >= 2:
                    dve.wait_ge(qk_done.sem, qk_done.at(layer, j - 1))
                marks = [0, 0]
                for k in range(MCONV_K):
                    for i in range(2):
                        s, c = 2 * (j % 2) + i, 2 * j + i
                        src, dst, tap = pre[:, s, k:k + T], cacc[:, s, :], col(2, R_MW + 16 * k + c)
                        if k:
                            ch.need(marks[i])
                            ins = dve.scalar_tensor_tensor(dst, src, tap, dst, ALU.mult, ALU.add)
                        else:
                            ins = dve.tensor_scalar(dst, src, tap, col(0, R_MB + c), ALU.mult, ALU.add)
                        if k == MCONV_K - 1 and i == 1:
                            ins.then_inc(qk_conv.sem, 1)
                        elif k < MCONV_K - 1:
                            marks[i] = ch.did(ins)

            def conv31(layer, j):
                for k in DVE_TAPS.get(j, ()):
                    marks = tap_marks
                    for i in range(2):
                        c = 2 + i
                        src, dst, tap = u_pad[:, c, k:k + T], c31[:, c, :], col(1, k * CB + c)
                        if k:
                            ch.need(marks[i])
                            ins = dve.scalar_tensor_tensor(dst, src, tap, dst, ALU.mult, ALU.add)
                        else:
                            ins = dve.tensor_scalar(dst, src, tap, col(0, R_CB + c), ALU.mult, ALU.add)
                        if k == CONV_K - 1 and i == 1:
                            ins.then_inc(c31_dve.sem, 1)
                        else:
                            marks[i] = ch.did(ins)

            def pooling(layer):
                dve.wait_ge(pool_pre.sem, pool_pre.at(layer, 2))
                sums = [dec[:, :, :].rearrange("p a b -> p (a b)"), wdk[:, :, :].rearrange("p a b -> p (a b)")]
                for g, win in enumerate(POOL_WINDOWS):
                    u = u_pool[:, g, :]
                    cur = u
                    for lev in range(g + 1):
                        sh = 1 << lev
                        nxt = sums[lev % 2]
                        ch.link(dve.tensor_tensor(nxt[:, 2 * sh - 1:271], cur[:, 2 * sh - 1:271], cur[:, sh - 1:271 - sh], ALU.add))
                        cur = nxt
                    ch.did(dve.scalar_tensor_tensor(pooled[:, g, :], cur[:, 15:271], 1.0 / win, u[:, 15:271], ALU.mult, ALU.subtract))
                    ch.link(dve.tensor_tensor(small[:, TMP:TMP + 16], cur[:, 15:31], rcnt[:, g, :], ALU.mult))
                    ins = dve.tensor_tensor(pooled[:, g, 0:16], small[:, TMP:TMP + 16], u[:, 15:31], ALU.subtract)
                    ch.link(ins) if g < NG - 1 else ins.then_inc(pool_done.sem, 1)

            def decayed_scores(layer, hd):
                dve.wait_ge(score_mul.sem, score_mul.at(layer, hd + 1))
                dve.wait_ge(dec_done.sem, dec_done.at(layer, hd + 1))
                if hd >= 2:
                    dve.wait_ge(num_mul.sem, num_mul.at(layer, hd - 1))
                dve.scalar_tensor_tensor(wdk[:, hd % 2, :], ps[5][:, 0:3 * P], DH ** -0.5, dec[:, hd % 2, :], ALU.mult, ALU.mult).then_inc(wdk_done.sem, 1)

            def hidden(layer, hd):
                dve.wait_ge(num_mul.sem, num_mul.at(layer, hd + 1))
                for tt in range(TT):
                    den, d = ps[6 + tt][:, DH:DH + 1], small[:, DEN + tt:DEN + tt + 1]
                    ch.link(dve.scalar_tensor_tensor(d, den, -1.0, gcols[:, 8 + 4 * tt + hd:9 + 4 * tt + hd], ALU.mult, ALU.max))
                    ch.link(dve.tensor_tensor(d, d, den, ALU.max))
                    ch.link(dve.reciprocal(d, d))
                    ins = dve.tensor_scalar(q_t[:, 2 * hd + tt, :], ps[6 + tt][:, 0:DH], d, None, ALU.mult)
                    ch.did(ins) if tt == 0 else ins.then_inc(hid_done.sem, 1)

            def merge(layer, j, n, parts):
                multiplied(layer, j)
                for i in range(parts):
                    dve.wait_ge(gate_done.sem, gate_done.at(layer, n + i + 1))
                    s, q = 2 * ((n + i) % 4), (n + i) % 4
                    g, y = flat(gates[:, s:s + 2, :]), flat(xf[:, 2 * q:2 * q + 2, :])
                    last = y_done if n >= 8 else gate_used
                    if n < 4:
                        if n == 0 and i == 0:
                            dve.wait_ge(c31_done.sem, c31_done.at(layer, 1))
                        dve.tensor_tensor(y, g, bank(("chunk", j), i)[:, :], ALU.mult).then_inc(last.sem, 1)
                    else:
                        ch.link(dve.tensor_tensor(g, g, bank(("chunk", j), i)[:, :], ALU.mult))
                        dve.tensor_tensor(y, y, g, ALU.add).then_inc(last.sem, 1)

            def residual(layer, j, i, done):
                multiplied(layer, j)
                s = flat(h[:, 2 * i:2 * i + 2, :])
                dve.tensor_tensor(s, s, bank(("chunk", j))[:, :], ALU.add).then_inc(done.sem, 1)

            def x_value(layer, j, hd):
                multiplied(layer, j)
                dve.tensor_copy(vx[:, :, hd, 0:DH], bank(("chunk", j))[:, :].rearrange("p (t e) -> p t e", t=TT)).then_inc(xv_done.sem, 1)

            def x_probs(layer, hd):
                dve.wait_ge(xs_mul.sem, xs_mul.at(layer, hd + 1))
                ch.link(dve.tensor_reduce(xcols[:, 2, hd, :], ps[4 + hd % 2][:, :].rearrange("p (t m) -> p t m", t=TT), AX, ALU.max))
                dve.tensor_scalar(xcols[:, 0, hd, :], xcols[:, 2, hd, :], -(DH ** -0.5), None, ALU.mult).then_inc(xmax.sem, 1)
                dve.wait_ge(xexp.sem, xexp.at(layer, hd + 1))
                ch.link(dve.reciprocal(xcols[:, 3, hd, :], xcols[:, 1, hd, :]))
                for tt in range(TT):
                    s = z_sig[:, 2 * (hd % 2) + tt, :]
                    ins = dve.tensor_scalar(s, s, xcols[:, 3, hd, tt:tt + 1], None, ALU.mult)
                ins.then_inc(xprob.sem, 1)

            def x_out(layer, hd):
                dve.wait_ge(xo_mul.sem, xo_mul.at(layer, hd + 1))
                dve.tensor_copy(flat(xf[:, 2 * hd:2 * hd + 2, :]), ps[7][:, :]).then_inc(xo_done.sem, 1)
                dve.wait_ge(xo_hi.sem, xo_hi.at(layer, hd + 1))
                lo(a_lo[:, 2 * hd:2 * hd + 2, :], xf[:, 2 * hd:2 * hd + 2, :], a_hi[:, 2 * hd:2 * hd + 2, :]).then_inc(xo_lo.sem, 1)

            def merged_lo(layer, q):
                dve.wait_ge(y_hi.sem, y_hi.at(layer, q + 1))
                lo(a_lo[:, 2 * q:2 * q + 2, :], xf[:, 2 * q:2 * q + 2, :], a_hi[:, 2 * q:2 * q + 2, :]).then_inc(y_lo.sem, 1)

            tap_marks = [0, 0]

            def post(layer, j):
                conv31(layer, j)
                if j == GATE_ROWS:
                    dve.wait_ge(if_mul.sem, if_mul.at(layer, 1))
                    dve.wait_ge(ifb_in.sem, ifb_in.at(layer, 32))
                    ch.did(dve.tensor_scalar(rows[:, 0, :], ps[5][0:HEADS, 0:T], if_bias[0:HEADS, :], None, ALU.add))
                    dve.tensor_scalar(rows[:, 1, :], ps[5][32:32 + HEADS, 0:T], if_bias[32:32 + HEADS, :], None, ALU.add).then_inc(if_dve.sem, 1)
                if QK0 <= j < V0:
                    conv4(layer, j - QK0)
                if j == GATE_ROWS + 1:
                    gate_scans(layer)
                if j == GATE_ROWS + 6:
                    dve.wait_ge(if_tr.sem, if_tr.at(layer, 1))
                    dve.tensor_copy(gcols[:, :], ps[6][:, 0:16]).then_inc(gcols_done.sem, 1)
                if V0 <= j < PU0:
                    hd = j - V0
                    multiplied(layer, j)
                    dve.wait_ge(vb_in.sem, vb_in.at(layer, 16))
                    for tt in range(TT):
                        ins = dve.tensor_tensor(vx[:, tt, hd, 0:DH], bank(("chunk", j))[:, tt * DH:(tt + 1) * DH], vb_pool[:, hd * DH:(hd + 1) * DH], ALU.add)
                    ins.then_inc(v_done.sem, 1)
                if j < QK0 and (j - AB0) % 2:
                    i = (j - AB0) // 2
                    multiplied(layer, j)
                    dve.wait_ge(b_sig.sem, b_sig.at(layer, i + 1))
                    for n in range(2):
                        ins = dve.scalar_tensor_tensor(u_pad[:, 2 * i + n, CONV_K - 1:], bank(("chunk", j))[:, n * HALF:(n + 1) * HALF],
                                                       col(0, C_A // P + 2 * i + n), sgb[:, n, :], ALU.add, ALU.mult)
                    ins.then_inc(u_done.sem, 1)
                if j == Z0 - 1:
                    pooling(layer)
                if j == Z0 + 1:
                    dve.wait_ge(pool_hi.sem, pool_hi.at(layer, 1))
                    lo(b_lo[:, 4:8, :], pooled, b_hi[:, 4:8, :]).then_inc(pool_lo.sem, 1)
                if j == PW:
                    multiplied(layer, j)
                    for g in range(NG):
                        ins = dve.tensor_scalar(pooled[:, g, :], bank(("chunk", j), g // 2)[:, (g % 2) * HALF:(g % 2 + 1) * HALF], col(0, R_PS + g), None, ALU.mult)
                    ins.then_inc(pw_done.sem, 1)
                    dve.wait_ge(pw_hi.sem, pw_hi.at(layer, 1))
                    lo(b_lo[:, 0:4, :], pooled, b_hi[:, 0:4, :]).then_inc(pw_lo.sem, 1)
                if j in SCORES:
                    decayed_scores(layer, SCORES.index(j))
                if j - 2 in SCORES:
                    hidden(layer, SCORES.index(j - 2))
                if j == SCORES[-1] + 3:
                    dve.wait_ge(hid_std.sem, hid_std.at(layer, 1))
                    ch.link(dve.reciprocal(small[:, RST:RST + 8], small[:, STD:STD + 8]))
                    for n in range(8):
                        ins = dve.tensor_scalar(q_t[:, n, :], q_t[:, n, :], small[:, RST + n:RST + n + 1], None, ALU.mult)
                    ins.then_inc(hid_nrm.sem, 1)
                if WP0 <= j < GA0:
                    merge(layer, j, 2 * (j - WP0), 2)
                if j == LN_MEAN:
                    dve.wait_ge(ln_sum.sem, ln_sum.at(layer, 1))
                    ch.link(dve.tensor_scalar(rstd[:, 1, :], ps[5][:, 0:T], 1.0 / CONV_W, None, ALU.mult))
                    for c in range(CB):
                        ins = dve.tensor_tensor(c31[:, c, :], c31[:, c, :], rstd[:, 1, :], ALU.subtract)
                    ins.then_inc(ln_cent.sem, 1)
                if j == LN_VAR:
                    dve.wait_ge(ln_std.sem, ln_std.at(layer, 1))
                    ch.link(dve.reciprocal(rstd[:, 1, :], rstd[:, 0, :]))
                    for c in range(CB):
                        ins = dve.scalar_tensor_tensor(c31[:, c, :], c31[:, c, :], col(0, R_LG + c), rstd[:, 1, :], ALU.mult, ALU.mult)
                    ins.then_inc(ln_nrm.sem, 1)
                    dve.wait_ge(ln_hi.sem, ln_hi.at(layer, 1))
                    lo(b_lo[:, 4:8, :], c31[:, :, :], b_hi[:, 4:8, :]).then_inc(ln_lo.sem, 1)
                if j == HIDDEN_T:
                    for hd in range(HEADS):
                        dve.wait_ge(hid_t.sem, hid_t.at(layer, hd + 1))
                        for e in range(2):
                            k = 2 * hd + e
                            ins = dve.scalar_tensor_tensor(k_t[:, k, :], bank("hidden_t", hd)[:, e * HALF:(e + 1) * HALF], col(2, R_MG + k),
                                                           z_sig[:, k, :], ALU.mult, ALU.mult)
                        ins.then_inc(hid_gated.sem, 1)
                if WC0 <= j < GC0:
                    merge(layer, j, 4 + 2 * (j - WC0), 2)
                if j == GC0 - 1:
                    for i in range(4):
                        dve.wait_ge(hid_hi.sem, hid_hi.at(layer, i + 1))
                        lo(b_lo[:, 2 * i:2 * i + 2, :], k_t[:, 2 * i:2 * i + 2, :], b_hi[:, 2 * i:2 * i + 2, :]).then_inc(hid_lo.sem, 1)
                if GC0 <= j < WO0 and (j - GC0) % 2:
                    merge(layer, j, 8 + (j - GC0) // 2, 1)
                if j == WO0 - 2:
                    for q in range(3):
                        merged_lo(layer, q)
                if j == WO0 - 1:
                    merged_lo(layer, 3)
                if WO0 <= j < XK0:
                    residual(layer, j, j - WO0, h_mix)
                if j == WO0:
                    for k in range(KB):
                        dve.wait_ge(mem_hi.sem, mem_hi.at(layer, k + 1))
                        dve.scalar_tensor_tensor(b_lo[:, k, :], mem_t[:, k, :], col(2, R_MEMG + k), as_f32(b_hi[:, k, :]), ALU.mult, ALU.subtract).then_inc(mem_lo.sem, 1)
                if j == XK0 + 1:
                    norm(layer, 1, R_NORM + 8, a_hi, a_lo)
                if j == XV0:
                    x_value(layer, j, 0)
                if XV1 <= j < XO0:
                    x_value(layer, j, j - XV1 + 1)
                if XQ0 <= j < XV1:
                    i = j - XQ0
                    multiplied(layer, j)
                    dve.tensor_copy(flat(q_t[:, 2 * i:2 * i + 2, :]), bank(("chunk", j))[:, :]).then_inc(xq_done.sem, 1)
                if XQ0 + 1 <= j < XQ0 + 1 + HEADS:
                    x_probs(layer, j - XQ0 - 1)
                for hd in X_OUT_AFTER.get(j, ()):
                    x_out(layer, hd)
                if XO0 <= j < N_MIX:
                    residual(layer, j, j - XO0, h_att)

            def ahead(layer, m):
                if layer == 0:
                    split(layer, N_MIX + m)
                else:
                    e_split(0, m)

            def mixer(layer):
                dve.wait_ge(par_t.sem, par_t.at(layer, 1))
                for j, n in enumerate(PAR_ROWS):
                    ins = dve.tensor_copy(par[:, j, 0:n], ps[3][:, j * P:j * P + n])
                ins.then_inc(par_c.sem, 1)
                dve.wait_ge(par_c.sem, par_c.at(layer, 1))
                if layer == 0:
                    split(layer, 0)
                norm(layer, 0, R_NORM, a_hi, a_lo)
                if layer:
                    split(layer, SPL - 1)
                dve.wait_ge(wif_split.sem, wif_split.at(layer, 1))
                lo(wif_lo[:, :, :], wif[:, :, :], wif_hi[:, :, :]).then_inc(wif_split.sem, 1)
                for c in range(SPL if layer else 1, N_MIX + SPL):
                    if c < N_MIX:
                        split(layer, c, chunk_len(c))
                    if c >= SPL:
                        post(layer, c - SPL)
                    if N_MIX <= c < N_MIX + SPL - 1:
                        ahead(layer, c - N_MIX)
                norm(layer, 2, R_NORM + 16, b_hi, b_lo)
                ahead(layer, SPL - 1)

            def dense(layer):
                def gated(g):
                    dve.wait_ge(ff_silu.sem, ff_silu.at(layer, g + 1))
                    multiplied(layer, N_MIX + FF_SEQ.index(("up", g, 1)))
                    s, d = 2 * (g % 2), 2 * (g % 4)
                    z = flat(z_sig[:, s:s + 2, :])
                    dve.tensor_tensor(z, z, ps[(2 * g + 1) % 4][:, :], ALU.mult).then_inc(ff_mul.sem, 1)
                    dve.wait_ge(ff_hi.sem, ff_hi.at(layer, g + 1))
                    lo(a_lo[:, d:d + 2, :], z_sig[:, s:s + 2, :], a_hi[:, d:d + 2, :]).then_inc(ff_lo.sem, 1)
                for c in range(SPL, N_FF + SPL):
                    if c < N_FF:
                        split(layer, N_MIX + c)
                    what, g, i = FF_SEQ[c - SPL]
                    if what == "up" and i == 1:
                        gated(g)
                    if N_FF <= c < N_FF + SPL - 1:
                        split(layer + 1, c - N_FF)
                multiplied(layer, N_LAYER - 1)
                for i in range(4):
                    s = flat(h[:, 2 * i:2 * i + 2, :])
                    dve.tensor_tensor(s, s, ps[4 + i][:, :], ALU.add).then_inc(h_ff.sem, 1)

            for i in range(4):
                dve.wait_ge(start_t, i + 1)
                dve.tensor_copy(flat(h[:, 2 * i:2 * i + 2, :]), ps[i][:, :]).then_inc(h_ff.sem, 1)
            for i in range(4):
                dve.wait_ge(start_t, 5 + i)
                dve.tensor_copy(flat(mem_t[:, 2 * i:2 * i + 2, :]), ps[i][:, :]).then_inc(start_c, 1)
            dve.wait_ge(start_c, 4)
            dve.wait_ge(std_done.sem, 1)
            ch.link(dve.reciprocal(rstd[:, 1, :], rstd[:, 0, :]))
            for k in range(KB):
                ins = dve.tensor_tensor(mem_t[:, k, :], mem_t[:, k, :], rstd[:, 1, :], ALU.mult)
                if k % 2:
                    ins.then_inc(xf_done.sem, 1)
            dve.sem_inc(lo_done.sem, RAW)
            dve.sem_inc(ln_lo.sem, 1)
            for layer in range(DEPTH):
                mixer(layer)
                if layer == 0:
                    dense(layer)
            def select(b):
                for tt in range(TT):
                    rank = x_rank[tt][:, bass.ds(b, 1)]
                    dve.tensor_scalar(sel[:, tt, :], iota_slot, rank, x_mask[tt][:, bass.ds(b, 1)], ALU.is_equal, ALU.mult)
                    ins = dve.tensor_scalar(sel_g[:, tt, :], iota_slot, rank, x_gate[tt][:, bass.ds(b, 1)], ALU.is_equal, ALU.mult)
                ins.then_inc(sel_done.sem, 1)

            def gather_lo(b):
                for i in range(2):
                    dve.wait_ge(x_hi_done.sem, x_hi_done.at(b, i + 1))
                    lo(x_lo[:, 4 * i:4 * i + 4, :].rearrange("p k s -> p (k s)"), ps[7 - i][:, :],
                       x_hi[:, 4 * i:4 * i + 4, :].rearrange("p k s -> p (k s)")).then_inc(x_lo_done.sem, 1)

            def e_post(b, m):
                kind, g, i = ESEQ[m]
                dve.wait_ge(e_pe.sem, e_pe.at(b, m + 1))
                if kind == "w3" and i == 1:
                    dve.wait_ge(e_silu.sem, e_silu.at(b, g + 1))
                    dve.tensor_tensor(act_e[g % 2], act_e[g % 2], ps[(2 * g + 1) % 4][:, :], ALU.mult).then_inc(e_gated.sem, 1)
                turned = {E_AT["w1", n + 1, 1]: n for n in range(NGE - 1)} | {E_AT["w2", NGE - 2, 1]: NGE - 1}
                if m in turned:
                    n = turned[m]
                    dve.wait_ge(e_hid_hi.sem, e_hid_hi.at(b, n + 1))
                    lo(hid_e[n % 2][1].rearrange("p k s -> p (k s)"), ps[6][:, :], hid_e[n % 2][0].rearrange("p k s -> p (k s)")).then_inc(e_hid_lo.sem, 1)
                if (kind, g, i) == ("w3", 1, 1):
                    dve.wait_ge(g_turned.sem, g_turned.at(b, 1))
                    dve.wait_ge(gathered.sem, gathered.at(b, 2))
                    select(b + 1)
                if m == E_AT["w2", NGE - 2, 1]:
                    gather_lo(b + 1)
                if m == N_EXP - 1:
                    for n in range(4):
                        dve.wait_ge(spread.sem, spread.at(b, n + 1))
                        t = flat(h[:, 2 * n:2 * n + 2, :])
                        dve.tensor_tensor(t, t, ps[(2 + n) % 4][:, :], ALU.add).then_inc(h_added.sem, 1)

            def e_block(b):
                for t in range(SPL, N_EXP + SPL):
                    if t < N_EXP:
                        e_split(b, t)
                    e_post(b, t - SPL)
                    if t >= N_EXP:
                        e_split(b + 1, t - N_EXP)

            def route():
                def both(step):
                    for tt in range(TT):
                        ins = step(tt, slice(tt, tt + 1))
                    ch.link(ins)
                dve.wait_ge(e_const, 5 + 3 * TT + 1)
                dve.wait_ge(logits_mul, 1)
                both(lambda tt, c: dve.tensor_copy(logit[tt], ps[5][:, tt * NE:(tt + 1) * NE]))
                for top, pick, one in ((best, pick1, oh1), (second, pick2, oh2)):
                    both(lambda tt, c: dve.tensor_reduce(top[:, c], logit[tt], AX, ALU.max))
                    both(lambda tt, c: dve.tensor_scalar(cand[tt], logit[tt], top[:, c], None, ALU.is_equal))
                    both(lambda tt, c: dve.scalar_tensor_tensor(cand[tt], cand[tt], -float(NE), iota8p, ALU.mult, ALU.add))
                    both(lambda tt, c: dve.tensor_reduce(pick[:, c], cand[tt], AX, ALU.min))
                    both(lambda tt, c: dve.tensor_scalar(one[tt], iota8, pick[:, c], None, ALU.is_equal))
                    if top is best:
                        both(lambda tt, c: dve.scalar_tensor_tensor(logit[tt], one[tt], -3e38, logit[tt], ALU.mult, ALU.add))
                dve.tensor_tensor(gap, second, best, ALU.subtract).then_inc(r_gap, 1)
                for tt in range(TT):
                    ins = dve.tensor_tensor(r_mask[tt], oh1[tt], oh2[tt], ALU.add)
                ins.then_inc(mask_done, 1)
                dve.wait_ge(r_exp, 1)
                ch.link(dve.tensor_scalar(g1, gap_e, 1.0, None, ALU.add))
                ch.link(dve.reciprocal(g1, g1))
                ch.link(dve.tensor_tensor(g2, gap_e, g1, ALU.mult))
                both(lambda tt, c: dve.tensor_scalar(r_gate[tt], oh1[tt], g1[:, c], None, ALU.mult))
                both(lambda tt, c: dve.scalar_tensor_tensor(r_gate[tt], oh2[tt], g2[:, c], r_gate[tt], ALU.mult, ALU.add))
                dve.wait_ge(rank_mul, 1)
                both(lambda tt, c: dve.tensor_copy(r_rank[tt], ps[5][:, 16 + tt * NE:16 + (tt + 1) * NE]))
                for to, of in ((x_rank, r_rank), (x_mask, r_mask), (x_gate, r_gate)):
                    both(lambda tt, c: dve.tensor_copy(to[tt][:, 0:NE], of[tt]))
                select(0)

            def further_blocks():
                ch.link(dve.tensor_copy(total, ps[5][:, 32:32 + NE]))
                ch.link(dve.tensor_scalar(over, total, float(SLOTS), None, ALU.is_gt))
                ch.link(dve.tensor_tensor_scan(incl, zero8, over, 0.0, ALU.add, ALU.add))
                ch.link(dve.tensor_tensor(excl, incl, over, ALU.subtract))
                for j in range(N_OVER):
                    ch.link(dve.scalar_tensor_tensor(over_oh[j], excl, float(j), over, ALU.is_equal, ALU.mult))
                    pairs = [(iota8, ids_f[:, NE + j:NE + j + 1])]
                    for tt in range(TT):
                        pairs += [(of[tt], to[tt][:, NE + j:NE + j + 1]) for to, of in ((x_rank, r_rank), (x_mask, r_mask), (x_gate, r_gate))]
                    for (of, to), prod in zip(pairs, prods):
                        ins = dve.tensor_tensor(prod, over_oh[j], of, ALU.mult)
                    ch.link(ins)
                    for (of, to), prod in zip(pairs, prods):
                        ins = dve.tensor_reduce(to, prod, AX, ALU.add)
                    ch.link(ins)
                    for tt in range(TT):
                        r = x_rank[tt][:, NE + j:NE + j + 1]
                        ins = dve.tensor_scalar(r, r, -float(SLOTS), None, ALU.add)
                    ch.link(ins)
                ch.link(dve.tensor_copy(ids_f[:, 0:NE], iota8))
                ch.link(dve.tensor_scalar(ids_f[:, NBLK + 1:NBLK + 2], incl[:, NE - 1:NE], float(NE), None, ALU.add))
                dve.tensor_copy(ids[0:1, :], ids_f[0:1, :]).then_inc(ids_done, 1)

            route()
            gather_lo(0)
            dve.sem_inc(h_added.sem, 4)
            further_blocks()
            with dve.Fori(0, NE) as b:
                e_block(b)
            dve.wait_ge(ids_done, 1)
            more = dve.value_load(ids[0:1, NBLK + 1:NBLK + 2], min_val=NE, max_val=NBLK)
            with dve.Fori(NE, NBLK) as b:
                with dve.If(b < more):
                    e_block(b)
            dve.drain().then_inc(settled, 1)
            dve.wait_ge(f_std, 1)
            ch.link(dve.reciprocal(rstd[:, 1, :], rstd[:, 0, :]))
            for k in range(KB):
                ins = dve.scalar_tensor_tensor(xf[:, k, :], h[:, k, :], col(2, R_FG + k), rstd[:, 1, :], ALU.mult, ALU.mult)
                if k % 4 == 3:
                    ins.then_inc(f_x, 1)

        @block.tensor
        def _(pe):
            def three(dst, wh, wl, xh, xl, start, stop):
                pe.matmul(dst, wh, xh, start=start, stop=False, skip_group_check=True)
                pe.matmul(dst, wh, xl, start=False, stop=False, skip_group_check=True)
                return pe.matmul(dst, wl, xh, start=False, stop=stop, skip_group_check=True)

            def take_banks(layer, key):
                for bank_no, before in PLAN[key]:
                    if before:
                        s, n = read_by(*before)
                        pe.wait_ge(s.sem, s.at(layer, n))

            def weights(c, k):
                return kn(w_hi[c % SPL], k), kn(w_lo[c % SPL], k)

            def project(layer, c, xh, xl, ready=None, blocks=KB, first=0):
                pe.wait_ge(lo_done.sem, lo_done.at(layer, c + 1))
                take_banks(layer, ("chunk", c))
                wh, wl = weights(c, blocks)
                outs = CH // blocks // P
                for k in range(blocks):
                    if ready and k % 2 == 0:
                        pe.wait_ge(ready[0].sem, ready[0].at(layer, ready[1] + k // 2 + 1))
                    for i in range(outs):
                        dst = bank(("chunk", c), i // 2)[:, (i % 2) * HALF:(i % 2 + 1) * HALF]
                        cols = slice(i * P, (i + 1) * P)
                        ins = three(dst, wh[:, k, cols], wl[:, k, cols], xh[:, first + k, :], xl[:, first + k, :],
                                    k == 0 and i % 2 == 0, k == blocks - 1)
                ins.then_inc(pe_chunk.sem, 1)

            def project_tokens(layer, c, xh, xl):
                pe.wait_ge(lo_done.sem, lo_done.at(layer, c + 1))
                take_banks(layer, ("chunk", c))
                wh, wl = weights(c, KB)
                for k in range(KB):
                    for tt in range(TT):
                        t = slice(tt * P, (tt + 1) * P)
                        ins = three(bank(("chunk", c))[:, tt * T:(tt + 1) * T], xh[:, k, t], xl[:, k, t], wh[:, k, :], wl[:, k, :],
                                    k == 0 and tt == 0, k == KB - 1)
                ins.then_inc(pe_chunk.sem, 1)

            def sum_squares(layer, n, j):
                pe.wait_ge(squared.sem, squared.at(layer, 4 * n + j + 1))
                for i in range(2):
                    ins = pe.matmul(ps[4][:, 0:T], ones[:, :], sq[:, j % 2, i * T:(i + 1) * T], start=(j == 0 and i == 0), stop=(j == 3 and i == 1),
                                    skip_group_check=True)
                ins.then_inc(summed.sem, 1)

            def input_forget(layer):
                pe.wait_ge(wif_split.sem, wif_split.at(layer, 2))
                pe.wait_ge(par_c.sem, par_c.at(layer, 1))
                for k in range(KB):
                    ins = three(ps[5][0:36, 0:T], wif_hi[:, k, :], wif_lo[:, k, :], a_hi[:, k, :], a_lo[:, k, :], k == 0, k == KB - 1)
                ins.then_inc(if_mul.sem, 1)

            def gate_columns(layer):
                pe.wait_ge(if_dve.sem, if_dve.at(layer, 2))
                pe.wait_ge(if_act.sem, if_act.at(layer, 2))
                for n, row in enumerate((0, 2)):
                    for tt in range(TT):
                        c = 8 * n + 4 * tt
                        ins = pe.transpose(ps[6][:, c:c + HEADS], rows[:, row, tt * P:(tt + 1) * P], ident[0:HEADS, 0:HEADS])
                ins.then_inc(if_tr.sem, 1)

            def scores(layer, hd):
                if hd:
                    pe.wait_ge(dec_exp.sem, dec_exp.at(layer, hd))
                    pe.wait_ge(wdk_done.sem, wdk_done.at(layer, hd))
                pe.matmul(ps[4][:, 0:T], selh[:, hd, :], m_row[:, :], start=True, stop=True).then_inc(m_bcast.sem, 1)
                pe.wait_ge(qk_done.sem, qk_done.at(layer, 8))
                for st, (c0, t0) in enumerate(((0, 0), (T, P))):
                    for e in range(2):
                        k = 2 * hd + e
                        ins = pe.matmul(ps[5][:, c0:c0 + T - t0], k_t[:, k, st * P:(st + 1) * P], q_t[:, k, t0:T],
                                        start=(st == 0 and e == 0), stop=(e == 1), skip_group_check=True)
                ins.then_inc(score_mul.sem, 1)

            def numerators(layer, hd):
                pe.wait_ge(wdk_done.sem, wdk_done.at(layer, hd + 1))
                if hd:
                    pe.wait_ge(hid_done.sem, hid_done.at(layer, hd))
                pe.wait_ge(v_done.sem, v_done.at(layer, HEADS))
                s = wdk[:, hd % 2, :]
                pe.matmul(ps[6][:, 0:DH + 1], s[:, 0:P], vx[:, 0, hd, :], start=True, stop=True)
                pe.matmul(ps[7][:, 0:DH + 1], s[:, P:T], vx[:, 0, hd, :], start=True, stop=False)
                pe.matmul(ps[7][:, 0:DH + 1], s[:, T:3 * P], vx[:, 1, hd, :], start=False, stop=True).then_inc(num_mul.sem, 1)

            def hidden_transpose(layer):
                pe.wait_ge(hid_nrm.sem, hid_nrm.at(layer, 1))
                take_banks(layer, "hidden_t")
                for hd in range(HEADS):
                    for e in range(2):
                        for tt in range(TT):
                            ins = pe.transpose(bank("hidden_t", hd)[:, e * T + tt * P:e * T + (tt + 1) * P],
                                               q_t[:, 2 * hd + tt, e * P:(e + 1) * P], ident[:, :])
                    ins.then_inc(hid_t.sem, 1)

            def ln_sums(layer, src, done):
                for c in range(CB):
                    ins = pe.matmul(ps[5][:, 0:T], ones[:, :], src[:, c, :], start=(c == 0), stop=(c == CB - 1))
                ins.then_inc(done.sem, 1)

            def x_scores(layer, hd):
                pe.wait_ge(xq_done.sem, xq_done.at(layer, hd + 1))
                pe.wait_ge(xk_done.sem, xk_done.at(layer, HEADS))
                if hd >= 2:
                    pe.wait_ge(xexp.sem, xexp.at(layer, hd - 1))
                for tt in range(TT):
                    for e in range(2):
                        k = 2 * hd + e
                        ins = pe.matmul(ps[4 + hd % 2][:, tt * T:(tt + 1) * T], q_t[:, k, tt * P:(tt + 1) * P], k_t[:, k, :],
                                        start=(tt == 0 and e == 0), stop=(e == 1), skip_group_check=True)
                ins.then_inc(xs_mul.sem, 1)

            def x_transpose(layer, hd):
                pe.wait_ge(xprob.sem, xprob.at(layer, hd + 1))
                if hd:
                    pe.wait_ge(xp_c.sem, xp_c.at(layer, hd))
                for m in range(TT):
                    for tt in range(TT):
                        ins = pe.transpose(ps[6][:, m * T + tt * P:m * T + (tt + 1) * P], z_sig[:, 2 * (hd % 2) + tt, m * P:(m + 1) * P], ident[:, :])
                ins.then_inc(xp_t.sem, 1)

            def x_output(layer, hd):
                pe.wait_ge(xp_c.sem, xp_c.at(layer, hd + 1))
                pe.wait_ge(xv_done.sem, xv_done.at(layer, hd + 1))
                if hd:
                    pe.wait_ge(xo_done.sem, xo_done.at(layer, hd))
                for e in range(2):
                    for m in range(TT):
                        ins = pe.matmul(ps[7][:, e * T:(e + 1) * T], vx[:, m, hd, e * P:(e + 1) * P], z_sig[:, 4 + 2 * (hd % 2) + m, :],
                                        start=(e == 0 and m == 0), stop=(m == 1), skip_group_check=True)
                ins.then_inc(xo_mul.sem, 1)

            def chunk(layer, c):
                if c < V0:
                    project(layer, c, a_hi, a_lo, (n_lo, 0) if c == 0 else None)
                elif c < PU0:
                    project_tokens(layer, c, a_hi, a_lo)
                elif c < PW or c in GATE_NO:
                    project(layer, c, a_hi, a_lo)
                elif c == PW:
                    pe.wait_ge(pool_lo.sem, pool_lo.at(layer, 1))
                    pe.wait_ge(lo_done.sem, lo_done.at(layer, c + 1))
                    take_banks(layer, ("chunk", c))
                    for g in range(NG):
                        n = slice(g * P, (g + 1) * P)
                        ins = three(bank(("chunk", c), g // 2)[:, (g % 2) * HALF:(g % 2 + 1) * HALF], w_hi[c % SPL][:, n], w_lo[c % SPL][:, n],
                                    b_hi[:, 4 + g, :], b_lo[:, 4 + g, :], g % 2 == 0, True)
                    ins.then_inc(pe_chunk.sem, 1)
                elif WP0 <= c < GA0:
                    pe.wait_ge(pw_lo.sem, pw_lo.at(layer, 1))
                    project(layer, c, b_hi, b_lo, None, CB, 0)
                elif WC0 <= c < GC0:
                    pe.wait_ge(ln_lo.sem, ln_lo.at(layer, 1))
                    project(layer, c, b_hi, b_lo, None, CB, CB)
                elif c < WO0:
                    project(layer, c, b_hi, b_lo, (hid_lo, 0))
                elif c < XK0:
                    project(layer, c, a_hi, a_lo, (y_lo, 0))
                elif c < XV0:
                    pe.wait_ge(mem_lo.sem, mem_lo.at(layer, KB))
                    project(layer, c, b_hi, b_lo)
                elif XQ0 <= c < XV1:
                    project(layer, c, a_hi, a_lo, (n_lo, 4))
                elif c < XO0:
                    project_tokens(layer, c, b_hi, b_lo)
                else:
                    project(layer, c, a_hi, a_lo, (xo_lo, 0))

            def mixer(layer):
                pe.wait_ge(par_in.sem, par_in.at(layer, 16 * 15))
                if layer:
                    pe.wait_ge(ff_mul.sem, ff_mul.at(0, N_FFG))
                else:
                    pe.wait_ge(start_c, 4)
                for j, n in enumerate(PAR_ROWS):
                    ins = pe.transpose(ps[3][:, j * P:j * P + n], prow[0:n, j, :], ident[0:n, 0:n])
                ins.then_inc(par_t.sem, 1)
                for j in range(4):
                    sum_squares(layer, 0, j)
                for c in range(N_MIX):
                    chunk(layer, c)
                    if c == GATE_ROWS:
                        input_forget(layer)
                    if c == GATE_ROWS + 6:
                        gate_columns(layer)
                    if c - 2 in SCORES:
                        numerators(layer, SCORES.index(c - 2))
                    if c in SCORES:
                        scores(layer, SCORES.index(c))
                    if c == LN_MEAN:
                        pe.wait_ge(c31_done.sem, c31_done.at(layer, 1))
                        pe.wait_ge(c31_dve.sem, c31_dve.at(layer, 1))
                        ln_sums(layer, c31, ln_sum)
                    if c == LN_VAR:
                        pe.wait_ge(ln_sq.sem, ln_sq.at(layer, 1))
                        ln_sums(layer, cacc, ln_var)
                    if c == HIDDEN_T:
                        hidden_transpose(layer)
                    if WO0 + 2 <= c < WO0 + 6:
                        sum_squares(layer, 1, c - WO0 - 2)
                    if XQ0 + 1 <= c < XQ0 + 1 + HEADS:
                        x_scores(layer, c - XQ0 - 1)
                    if XQ0 + 2 <= c < XQ0 + 2 + HEADS:
                        x_transpose(layer, c - XQ0 - 2)
                    for hd in X_OUT_AFTER.get(c, ()):
                        x_output(layer, hd)
                    if c >= XO0 + 2:
                        sum_squares(layer, 2, c - XO0 - 2)
                for j in (2, 3):
                    sum_squares(layer, 2, j)

            def dense(layer):
                for j, (what, g, i) in enumerate(FF_SEQ):
                    c = N_MIX + j
                    if what == "up":
                        pe.wait_ge(lo_done.sem, lo_done.at(layer, c + 1))
                        if g >= 2:
                            s = (ff_silu, ff_mul)[i]
                            pe.wait_ge(s.sem, s.at(layer, g - 1))
                        wh, wl = weights(c, KB)
                        b = ps[(2 * g + i) % 4]
                        for k in range(KB):
                            if j == 0 and k % 2 == 0:
                                pe.wait_ge(n_lo.sem, n_lo.at(layer, 8 + k // 2 + 1))
                            for n in range(2):
                                cols = slice(n * P, (n + 1) * P)
                                ins = three(b[:, n * HALF:(n + 1) * HALF], wh[:, k, cols], wl[:, k, cols], b_hi[:, k, :], b_lo[:, k, :],
                                            k == 0 and n == 0, k == KB - 1)
                    else:
                        pe.wait_ge(lo_done.sem, lo_done.at(layer, c + 1))
                        pe.wait_ge(ff_lo.sem, ff_lo.at(layer, g + 1))
                        wh, wl = weights(c, 2)
                        for k in range(2):
                            x = 2 * (g % 4) + k
                            for n in range(KB):
                                cols = slice(n * P, (n + 1) * P)
                                ins = three(ps[4 + n // 2][:, (n % 2) * HALF:(n % 2 + 1) * HALF], wh[:, k, cols], wl[:, k, cols],
                                            a_hi[:, x, :], a_lo[:, x, :], g == 0 and k == 0 and n % 2 == 0, g == N_FFG - 1 and k == 1)
                    ins.then_inc(pe_chunk.sem, 1)

            pe.wait_ge(const_done, CONSTS)
            for n in range(2):
                pe.wait_ge(x_in[n], 16)
                src = (q_t, k_t)[n]
                for i in range(4):
                    if n:
                        pe.wait_ge(h_ff.sem, i + 1)
                    for dd in range(2):
                        for tt in range(TT):
                            k = 2 * i + dd
                            ins = pe.transpose(ps[i][:, dd * T + tt * P:dd * T + (tt + 1) * P], src[:, 4 * tt + k // 2, (k % 2) * P:(k % 2 + 1) * P], ident[:, :])
                    ins.then_inc(start_t, 1)
            for j in range(4):
                pe.wait_ge(squared.sem, j + 1)
                for i in range(2):
                    ins = pe.matmul(ps[4][:, 0:T], ones[:, :], sq[:, j % 2, i * T:(i + 1) * T], start=(j == 0 and i == 0), stop=(j == 3 and i == 1),
                                    skip_group_check=True)
                ins.then_inc(summed.sem, 1)
            pe.sem_inc(pe_chunk.sem, SPL)
            pe.sem_inc(e_pe.sem, SPL)
            for layer in range(DEPTH):
                mixer(layer)
                if layer == 0:
                    dense(layer)
            pe.wait_ge(xf_done.sem, xf_done.moe)
            pe.wait_ge(rw_in, 16)
            for tt in range(TT):
                for k in range(KB):
                    ins = pe.matmul(ps[5][:, tt * NE:(tt + 1) * NE], xf[:, k, tt * P:(tt + 1) * P], rw[:, k, :],
                                    start=(tt == 0 and k == 0), stop=(k == KB - 1), skip_group_check=True)
            ins.then_inc(logits_mul, 1)

            def by_token(done):
                for i in range(4):
                    for k in range(4):
                        ins = pe.transpose(ps[i][:, k * P:(k + 1) * P], xf[:, 4 * (i % 2) + k, (i // 2) * P:(i // 2 + 1) * P], ident[:, :])
                    ins.then_inc(done, 1)
            by_token(tok_t)
            pe.wait_ge(mask_done, 1)
            pe.wait_ge(e_const, 5)
            for n, (lhs, tt, first, last) in enumerate(((before, 0, True, True), (ones[:, :], 0, True, False), (before, 1, False, True),
                                                        (ones[:, :], 0, True, False), (ones[:, :], 1, False, True))):
                c = 16 + NE * (0, 1, 1, 2, 2)[n]
                ins = pe.matmul(ps[5][:, c:c + NE], lhs, r_mask[tt], start=(n == 0), stop=last, skip_group_check=True)
            ins.then_inc(rank_mul, 1)

            def gather(b):
                pe.wait_ge(sel_done.sem, sel_done.at(b, 1))
                for i in range(2):
                    for k in range(4):
                        for tt in range(TT):
                            c = (4 * i + k) * P
                            ins = pe.matmul(ps[7 - i][:, k * P:(k + 1) * P], h_tok[:, tt, c:c + P], sel[:, tt, :],
                                            start=(k == 0 and tt == 0), stop=(tt == 1), skip_group_check=True)
                    ins.then_inc(gathered.sem, 1)

            def turn(b, g):
                pe.wait_ge(e_gated.sem, e_gated.at(b, g + 1))
                if g:
                    pe.wait_ge(e_hid_lo.sem, e_hid_lo.at(b, g))
                for k in range(4):
                    ins = pe.transpose(ps[6][:, k * P:(k + 1) * P], act_e[g % 2][:, k * P:(k + 1) * P], ident[:, :])
                ins.then_inc(e_turned.sem, 1)

            def e_chunk(b, m):
                kind, g, i = ESEQ[m]
                pe.wait_ge(e_lo.sem, e_lo.at(b, m + 1))
                wh, wl = w_hi[m % SPL], w_lo[m % SPL]
                if kind == "w2":
                    if i == 0:
                        pe.wait_ge(e_hid_lo.sem, e_hid_lo.at(b, g + 1))
                        if g == 0:
                            pe.wait_ge(y_copied.sem, y_copied.at(b, 0))
                    xh, xl = hid_e[g % 2]
                    for k in range(2):
                        for n in range(2):
                            c = slice(k * D + n * 512, k * D + (n + 1) * 512)
                            ins = three(ps[4 + n][:, :], xh[:, 2 * i + k, :], xl[:, 2 * i + k, :], wh[:, c], wl[:, c],
                                        g == 0 and i == 0 and k == 0, g == NGE - 1 and i == 1 and k == 1)
                else:
                    up = kind == "w3"
                    if i == 0:
                        if g == 0:
                            pe.wait_ge(h_added.sem, h_added.at(b, up - 1))
                        elif g > 1:
                            s = (e_silu, e_gated)[up]
                            pe.wait_ge(s.sem, s.at(b, g - 1))
                    if g == 0 and not up:
                        pe.wait_ge(x_lo_done.sem, x_lo_done.at(b, i + 1))
                    for k in range(4):
                        c = slice(k * FG, (k + 1) * FG)
                        ins = three(ps[(2 * g + up) % 4][:, :], x_hi[:, 4 * i + k, :], x_lo[:, 4 * i + k, :], wh[:, c], wl[:, c],
                                    i == 0 and k == 0, i == 1 and k == 3)
                ins.then_inc(e_pe.sem, 1)

            def e_block(b):
                for m, (kind, g, i) in enumerate(ESEQ):
                    e_chunk(b, m)
                    if (kind, g, i) == ("w3", 0, 1):
                        for tt in range(TT):
                            ins = pe.transpose(ps[7][:, tt * P:(tt + 1) * P], sel_g[:, tt, :], ident[:, :])
                        ins.then_inc(g_turned.sem, 1)
                    if kind == "w1" and i == 1 and g:
                        turn(b, g - 1)
                    if (kind, g, i) == ("w2", NGE - 2, 1):
                        turn(b, NGE - 1)
                        pe.wait_ge(g_copied.sem, g_copied.at(b, 1))
                        gather_next(b)
                pe.wait_ge(y_copied.sem, y_copied.at(b, 1))
                for n in range(4):
                    for i in range(2):
                        c = (2 * n + i) * P
                        ins = pe.matmul(ps[(2 + n) % 4][:, i * T:(i + 1) * T], y_tok[:, c:c + P], g_slot, start=(i == 0), stop=True,
                                        skip_group_check=True)
                    ins.then_inc(spread.sem, 1)

            def gather_next(b):
                pe.wait_ge(sel_done.sem, sel_done.at(b + 1, 1))
                for i in range(2):
                    if i:
                        pe.wait_ge(e_hid_lo.sem, e_hid_lo.at(b, NGE))
                    for k in range(4):
                        for tt in range(TT):
                            c = (4 * i + k) * P
                            ins = pe.matmul(ps[7 - i][:, k * P:(k + 1) * P], h_tok[:, tt, c:c + P], sel[:, tt, :],
                                            start=(k == 0 and tt == 0), stop=(tt == 1), skip_group_check=True)
                    ins.then_inc(gathered.sem, 1)

            pe.wait_ge(tok_c, 4)
            gather(0)
            with pe.Fori(0, NE) as b:
                e_block(b)
            pe.wait_ge(ids_done, 1)
            more = pe.value_load(ids[0:1, NBLK + 1:NBLK + 2], min_val=NE, max_val=NBLK)
            with pe.Fori(NE, NBLK) as b:
                with pe.If(b < more):
                    e_block(b)
            pe.drain().then_inc(settled, 1)
            pe.wait_ge(settled, 3)
            for j in range(4):
                pe.wait_ge(f_sq, j + 1)
                for i in range(2):
                    ins = pe.matmul(ps[4][:, 0:T], ones[:, :], sq[:, j % 2, i * T:(i + 1) * T], start=(j == 0 and i == 0), stop=(j == 3 and i == 1),
                                    skip_group_check=True)
                ins.then_inc(f_sum, 1)
            pe.wait_ge(f_x, 2)
            by_token(f_t)

    return nc


_INS = ['x', 'mem', 'mem_norm_g', 'norm_mix_g', 'w_in', 'b_in', 'conv_dw_w', 'conv_dw_b', 'conv_ln_g', 'conv_ln_b', 'w_conv_out',
        'pool_w', 'pool_scale', 'w_pool_out', 'mlstm_conv_w', 'mlstm_conv_b', 'mlstm_norm_g', 'w_mlstm_out', 'w_out',
        'norm_xattn_g', 'xa_wq', 'xa_wk', 'xa_wv', 'xa_wo', 'norm_ffn_g', 'ffn_w1', 'ffn_w3', 'ffn_w2', 'router_w',
        'moe_w1', 'moe_w3', 'moe_w2', 'final_norm_g']


def kernel(**inputs):
    import numpy as _np
    import concourse.bacc as _bacc
    from concourse.bass_utils import run_bass_kernel_spmd as _run

    nc = _bacc.Bacc("TRN2", target_bir_lowering=False, num_devices=1)
    arrays, args = {}, {}
    for name in _INS:
        a = _np.ascontiguousarray(inputs[name])
        arrays[f"in_{name}"] = a
        args[name] = nc.dram_tensor(f"in_{name}", a.shape, mybir.dt.from_np(a.dtype), kind="ExternalInput").ap()
    out = nc.dram_tensor("out_0", (1, T, D), F32, kind="ExternalOutput").ap()
    trunk(nc, args, out)
    r = _run(nc, [arrays], core_ids=[0])
    return r.results[0]["out_0"]
```
